# Optimizing a Trainium2 kernel written in Bass

```python
import jax, jax.numpy as jnp
from jax import lax
import numpy as np

D_MODEL = 2048
BATCH = 1
SEQ = 256
DEPTH = 1

HEAD_DIM = 128
ATTN_Q_HEADS = 8
ATTN_KV_HEADS = 2
ATTN_GROUP = ATTN_Q_HEADS // ATTN_KV_HEADS
WINDOW = 128
ATTN_BLOCK = 128
ROPE_THETA = 10000.0
RET_HEADS = 8
RET_QK_DIM = 128
RET_V_DIM = 256
RET_CHUNK = 128
PEER_HEADS = 8
PEER_N_KEYS = 128
PEER_N_EXPERTS = PEER_N_KEYS * PEER_N_KEYS
PEER_TOPK = 16
PEER_KEY_DIM = 256
PEER_HALF_DIM = PEER_KEY_DIM // 2
PEER_TOKEN_BLOCK = 128
NORM_EPS = 1e-6

ATTN_Q_W = ATTN_Q_HEADS * HEAD_DIM
ATTN_KV_W = ATTN_KV_HEADS * HEAD_DIM
RET_QK_W = RET_HEADS * RET_QK_DIM
RET_V_W = RET_HEADS * RET_V_DIM
IN_WIDTHS = (ATTN_Q_W, ATTN_KV_W, ATTN_KV_W, RET_QK_W, RET_QK_W, RET_V_W, RET_V_W, D_MODEL, D_MODEL)
IN_WIDTH = ATTN_Q_W + 2 * ATTN_KV_W + 2 * RET_QK_W + 2 * RET_V_W + 2 * D_MODEL


def _split_points():
    pts, acc = [], 0
    for w in IN_WIDTHS[:-1]:
        acc += w
        pts.append(acc)
    return pts

def rmsnorm(x, g):
    xf = x.astype(jnp.float32)
    y = xf * lax.rsqrt(jnp.mean(xf * xf, axis=-1, keepdims=True) + NORM_EPS)
    return (y * g.astype(jnp.float32)).astype(x.dtype)

def rope_tables(seq):
    pos = jnp.arange(seq, dtype=jnp.float32)
    inv_freq = 1.0 / (ROPE_THETA ** (jnp.arange(0, HEAD_DIM, 2, dtype=jnp.float32) / HEAD_DIM))
    ang = pos[:, None] * inv_freq[None, :]
    return jnp.cos(ang)[:, None, :], jnp.sin(ang)[:, None, :]

def apply_rope(x, cos, sin):
    cos = cos.astype(x.dtype)
    sin = sin.astype(x.dtype)
    x1, x2 = jnp.split(x, 2, axis=-1)
    return jnp.concatenate([x1 * cos - x2 * sin, x2 * cos + x1 * sin], axis=-1)

def sliding_window_attention(q, k, v, sinks, cos, sin):
    B, S, _ = q.shape
    C = ATTN_BLOCK
    N = S // C
    q = apply_rope(q.reshape(B, S, ATTN_Q_HEADS, HEAD_DIM), cos, sin)
    k = apply_rope(k.reshape(B, S, ATTN_KV_HEADS, HEAD_DIM), cos, sin)
    v = v.reshape(B, S, ATTN_KV_HEADS, HEAD_DIM)
    qb = q.reshape(B, N, C, ATTN_KV_HEADS, ATTN_GROUP, HEAD_DIM)

    def banded(t):
        tb = t.reshape(B, N, C, ATTN_KV_HEADS, HEAD_DIM)
        prev = jnp.concatenate([jnp.zeros_like(tb[:, :1]), tb[:, :-1]], axis=1)
        return jnp.concatenate([prev, tb], axis=2)

    kb, vb = banded(k), banded(v)
    scores = jnp.einsum('bnqhgd,bnkhd->bhgnqk', qb, kb).astype(jnp.float32) * (HEAD_DIM ** -0.5)
    qi = jnp.arange(C)[:, None]
    kj = jnp.arange(2 * C)[None, :]
    diff = qi + C - kj
    blk = jnp.arange(N)[:, None, None]
    allowed = (diff >= 0) & (diff < WINDOW) & ((blk > 0) | (kj >= C))
    scores = jnp.where(allowed, scores, jnp.float32(-1e30))
    sink = sinks.astype(jnp.float32).reshape(ATTN_KV_HEADS, ATTN_GROUP)[None, :, :, None, None, None]
    sink = jnp.broadcast_to(sink, scores.shape[:-1] + (1,))
    probs = jax.nn.softmax(jnp.concatenate([scores, sink], axis=-1), axis=-1)[..., :-1]
    out = jnp.einsum('bhgnqk,bnkhd->bnqhgd', probs.astype(v.dtype), vb)
    return out.reshape(B, S, ATTN_Q_W)

def retention(q, k, v, g, cos, sin):
    B, S, _ = q.shape
    C = RET_CHUNK
    N = S // C
    H = RET_HEADS
    q = apply_rope(q.reshape(B, S, H, RET_QK_DIM), cos, sin)
    k = apply_rope(k.reshape(B, S, H, RET_QK_DIM), cos, sin) * (RET_QK_DIM ** -0.5)
    v = v.reshape(B, S, H, RET_V_DIM)
    qc = q.reshape(B, N, C, H, RET_QK_DIM).transpose(0, 3, 1, 2, 4).astype(jnp.float32)
    kc = k.reshape(B, N, C, H, RET_QK_DIM).transpose(0, 3, 1, 2, 4).astype(jnp.float32)
    vc = v.reshape(B, N, C, H, RET_V_DIM).transpose(0, 3, 1, 2, 4).astype(jnp.float32)

    log_gamma = jnp.log(1.0 - 2.0 ** (-5.0 - jnp.arange(H, dtype=jnp.float32)))
    pos = jnp.arange(C, dtype=jnp.float32)
    d = pos[:, None] - pos[None, :]
    decay_mask = jnp.where(d >= 0, jnp.exp(log_gamma[:, None, None] * jnp.maximum(d, 0.0)), 0.0)
    inner = jnp.einsum('bhncd,bhnkd->bhnck', qc, kc) * decay_mask[None, :, None]
    o_intra = jnp.einsum('bhnck,bhnke->bhnce', inner, vc)

    k_decay = jnp.exp(log_gamma[:, None] * (C - 1.0 - pos)[None, :])
    q_decay = jnp.exp(log_gamma[:, None] * (pos + 1.0)[None, :])
    chunk_decay = jnp.exp(log_gamma * C)
    kv = jnp.einsum('bhnkd,bhnke->bhnde', kc * k_decay[None, :, None, :, None], vc)

    def step(state, kv_n):
        return state * chunk_decay[None, :, None, None] + kv_n, state

    init = jnp.zeros((B, H, RET_QK_DIM, RET_V_DIM), jnp.float32)
    _, prev_states = lax.scan(step, init, kv.transpose(2, 0, 1, 3, 4))
    prev_states = prev_states.transpose(1, 2, 0, 3, 4)
    o_cross = jnp.einsum('bhncd,bhnde->bhnce', qc * q_decay[None, :, None, :, None], prev_states)
    o = (o_intra + o_cross).transpose(0, 2, 3, 1, 4).reshape(B, S, H, RET_V_DIM)
    mu = jnp.mean(o, axis=-1, keepdims=True)
    var = jnp.mean(jnp.square(o - mu), axis=-1, keepdims=True)
    o = ((o - mu) * lax.rsqrt(var + NORM_EPS)).astype(g.dtype).reshape(B, S, RET_V_W)
    return o * jax.nn.silu(g)

def peer(x, w_query, sub_keys, expert_down, expert_up):
    B, S, D = x.shape
    T = B * S
    H, K = PEER_HEADS, PEER_TOPK
    xt = x.reshape(T, D)
    qry = (xt @ w_query).reshape(T, H, 2, PEER_HALF_DIM)
    s = jnp.einsum('thpd,phnd->thpn', qry, sub_keys).astype(jnp.float32)
    top_s, top_i = lax.top_k(s, K)
    cand_s = top_s[:, :, 0, :, None] + top_s[:, :, 1, None, :]
    cand_i = top_i[:, :, 0, :, None] * PEER_N_KEYS + top_i[:, :, 1, None, :]
    best_s, best_pos = lax.top_k(cand_s.reshape(T, H, K * K), K)
    expert_idx = jnp.take_along_axis(cand_i.reshape(T, H, K * K), best_pos, axis=-1)
    gates = jax.nn.softmax(best_s, axis=-1).astype(x.dtype)
    nb = T // PEER_TOKEN_BLOCK

    def block(args):
        xb, ib, gb = args
        u = expert_down[ib]
        act = jax.nn.gelu(jnp.einsum('td,thkd->thk', xb, u), approximate=False)
        vv = expert_up[ib]
        return jnp.einsum('thk,thkd->td', gb * act, vv)

    y = lax.map(block, (xt.reshape(nb, PEER_TOKEN_BLOCK, D),
                        expert_idx.reshape(nb, PEER_TOKEN_BLOCK, H, K),
                        gates.reshape(nb, PEER_TOKEN_BLOCK, H, K)))
    return y.reshape(B, S, D)

def first_inputs(seed: int = 0) -> dict:
    key = jax.random.key(seed)
    ks = jax.random.split(key, 14)
    f32 = jnp.float32
    L, D = DEPTH, D_MODEL
    nrm = lambda k, shape, scale: jax.random.normal(k, shape, f32) * scale
    return {
        "x": jax.random.normal(ks[0], (BATCH, SEQ, D), f32),
        "attn_norm": 1.0 + nrm(ks[1], (L, D), 0.02),
        "w_in": nrm(ks[2], (L, D, IN_WIDTH), D ** -0.5),
        "attn_sinks": nrm(ks[3], (L, ATTN_Q_HEADS), 0.5),
        "w_attn_branch": nrm(ks[4], (L, ATTN_Q_W, D), ATTN_Q_W ** -0.5),
        "w_ret_branch": nrm(ks[5], (L, RET_V_W, D), RET_V_W ** -0.5),
        "w_out": nrm(ks[6], (L, D, D), D ** -0.5),
        "ffn_norm": 1.0 + nrm(ks[7], (L, D), 0.02),
        "w_peer_query": nrm(ks[8], (L, D, PEER_HEADS * PEER_KEY_DIM), D ** -0.5),
        "peer_sub_keys": nrm(ks[9], (L, 2, PEER_HEADS, PEER_N_KEYS, PEER_HALF_DIM), PEER_HALF_DIM ** -0.5),
        "peer_expert_down": nrm(ks[10], (L, PEER_N_EXPERTS, D), D ** -0.5),
        "peer_expert_up": nrm(ks[11], (L, PEER_N_EXPERTS, D), PEER_HEADS ** -0.5),
        "final_norm": 1.0 + nrm(ks[12], (D,), 0.02),
    }

def first_block(x, attn_norm, w_in, attn_sinks, w_attn_branch, w_ret_branch, w_out, ffn_norm,
              w_peer_query, peer_sub_keys, peer_expert_down, peer_expert_up, final_norm):
    S = x.shape[1]
    cos, sin = rope_tables(S)
    splits = _split_points()
    h = x
    for layer in range(DEPTH):
        xn = rmsnorm(h, attn_norm[layer])
        proj = xn @ w_in[layer]
        q_a, k_a, v_a, q_r, k_r, v_r, g_r, gate_a, gate_r = jnp.split(proj, splits, axis=-1)
        y_a = sliding_window_attention(q_a, k_a, v_a, attn_sinks[layer], cos, sin) @ w_attn_branch[layer]
        y_r = retention(q_r, k_r, v_r, g_r, cos, sin) @ w_ret_branch[layer]
        merged = jax.nn.sigmoid(gate_a) * y_a + jax.nn.sigmoid(gate_r) * y_r
        h = h + merged @ w_out[layer]
        hn = rmsnorm(h, ffn_norm[layer])
        h = h + peer(hn, w_peer_query[layer], peer_sub_keys[layer],
                     peer_expert_down[layer], peer_expert_up[layer])
    return rmsnorm(h, final_norm)


D_MIX = D_MODEL
ATT_HEADS = (D_MIX // 2) // HEAD_DIM
D_ATT = ATT_HEADS * HEAD_DIM
D_RNN = D_MIX - D_ATT
RNN_BLOCKS = 8
RNN_BLOCK = D_RNN // RNN_BLOCKS
CONV_WIDTH = 4
LRU_C = 8.0
Q_BLOCK = 128
COL_Q = 0
COL_K = COL_Q + D_ATT
COL_V = COL_K + D_ATT
COL_F = COL_V + D_ATT
COL_RX = COL_F + ATT_HEADS
COL_RG = COL_RX + D_RNN
D_IN_PROJ = COL_RG + D_RNN
N_GROUPS = 4
EXPERTS_PER_GROUP = 8
N_EXPERTS = N_GROUPS * EXPERTS_PER_GROUP
TOP_K_INNER = 2
D_EXPERT = D_MODEL // 8
D_PLE = 256
FORGET_BIAS_INIT = 2.0
EPS = 1e-6


def rms_norm(x, gain):
    x32 = x.astype(jnp.float32)
    y = x32 * lax.rsqrt(jnp.mean(x32 * x32, axis=-1, keepdims=True) + EPS)
    return (y * gain.astype(jnp.float32)).astype(x.dtype)

def forgetting_attention(q, k, v, log_f):
    b, s, h, dh = q.shape
    nb = s // Q_BLOCK
    scale = dh ** -0.5
    c = jnp.cumsum(log_f, axis=1).transpose(0, 2, 1)
    kh = k.transpose(0, 2, 1, 3)
    vh = v.transpose(0, 2, 1, 3)
    q_blocks = q.transpose(0, 2, 1, 3).reshape(b, h, nb, Q_BLOCK, dh).transpose(2, 0, 1, 3, 4)
    c_blocks = c.reshape(b, h, nb, Q_BLOCK).transpose(2, 0, 1, 3)
    k_pos = jnp.arange(s, dtype=jnp.int32)
    starts = jnp.arange(nb, dtype=jnp.int32) * Q_BLOCK

    def one_block(args):
        qb, cb, start = args
        logits = jnp.einsum('bhqd,bhkd->bhqk', qb, kh,
                            preferred_element_type=jnp.float32) * scale
        logits = logits + cb[..., :, None] - c[:, :, None, :]
        q_pos = start + jnp.arange(Q_BLOCK, dtype=jnp.int32)
        causal = k_pos[None, :] <= q_pos[:, None]
        logits = jnp.where(causal, logits, -jnp.inf)
        probs = jax.nn.softmax(logits, axis=-1)
        return jnp.einsum('bhqk,bhkd->bhqd', probs.astype(vh.dtype), vh)

    out = lax.map(one_block, (q_blocks, c_blocks, starts))
    return out.transpose(1, 0, 3, 2, 4).reshape(b, s, h * dh)

def causal_depthwise_conv(x, w, bias):
    y = lax.conv_general_dilated(
        x, w[:, None, :].astype(x.dtype), window_strides=(1,),
        padding=[(CONV_WIDTH - 1, 0)],
        dimension_numbers=('NWC', 'WIO', 'NWC'),
        feature_group_count=x.shape[-1])
    return y + bias

def rg_lru(x, w_a, b_a, w_i, b_i, lam):
    b, s, d = x.shape
    xb = x.reshape(b, s, RNN_BLOCKS, RNN_BLOCK)
    r = jax.nn.sigmoid(jnp.einsum('bsni,nij->bsnj', xb, w_a).reshape(b, s, d) + b_a)
    i = jax.nn.sigmoid(jnp.einsum('bsni,nij->bsnj', xb, w_i).reshape(b, s, d) + b_i)
    log_a = -LRU_C * r.astype(jnp.float32) * jax.nn.softplus(-lam.astype(jnp.float32))
    a = jnp.exp(log_a)
    u = jnp.sqrt(-jnp.expm1(2.0 * log_a)) * (i * x).astype(jnp.float32)

    def combine(left, right):
        a1, b1 = left
        a2, b2 = right
        return a1 * a2, a2 * b1 + b2

    _, h = lax.associative_scan(combine, (a, u), axis=1)
    return h.astype(x.dtype)

def hierarchical_moe(hn, w_router_group, w_router_expert, w_gate, w_up, w_down):
    b, s, d = hn.shape
    t = hn.reshape(b * s, d)
    g_probs = jax.nn.softmax(jnp.dot(t, w_router_group, preferred_element_type=jnp.float32), axis=-1)
    g_w, g_idx = lax.top_k(g_probs, 1)
    e_logits = jnp.dot(t, w_router_expert, preferred_element_type=jnp.float32)
    e_logits = e_logits.reshape(-1, N_GROUPS, EXPERTS_PER_GROUP)
    e_in_group = jnp.take_along_axis(e_logits, g_idx[:, :, None], axis=1)[:, 0]
    top_l, top_i = lax.top_k(e_in_group, TOP_K_INNER)
    weights = jax.nn.softmax(top_l, axis=-1) * g_w
    ids = g_idx * EXPERTS_PER_GROUP + top_i
    comb = jnp.sum(jax.nn.one_hot(ids, N_EXPERTS, dtype=jnp.float32) * weights[..., None], axis=1)
    out = jnp.zeros((b * s, d), jnp.float32)
    for e in range(N_EXPERTS):
        hid = jax.nn.silu(t @ w_gate[e]) * (t @ w_up[e])
        out = out + (hid @ w_down[e]).astype(jnp.float32) * comb[:, e:e + 1]
    return out.astype(hn.dtype).reshape(b, s, d)

def second_inputs(seed: int = 0) -> dict:
    key = jax.random.key(seed)
    ks = jax.random.split(key, 32)
    f32 = jnp.float32

    def nrm(k, shape, scale):
        return jax.random.normal(k, shape, f32) * scale

    def gain(k, shape):
        return 1.0 + 0.02 * jax.random.normal(k, shape, f32)

    u = jax.random.uniform(ks[12], (DEPTH, D_RNN), f32, 0.9, 0.999)
    s_lam = u ** (1.0 / LRU_C)
    lru_lambda = jnp.log(s_lam) - jnp.log1p(-s_lam)
    return {
        "x": nrm(ks[0], (BATCH, SEQ, D_MODEL), 1.0),
        "p": nrm(ks[1], (DEPTH, BATCH, SEQ, D_PLE), 1.0),
        "mix_norm": gain(ks[2], (DEPTH, D_MODEL)),
        "w_in": nrm(ks[3], (DEPTH, D_MODEL, D_IN_PROJ), D_MODEL ** -0.5),
        "b_forget": FORGET_BIAS_INIT + 0.1 * jax.random.normal(ks[4], (DEPTH, ATT_HEADS), f32),
        "q_norm": gain(ks[5], (DEPTH, HEAD_DIM)),
        "k_norm": gain(ks[6], (DEPTH, HEAD_DIM)),
        "conv_w": nrm(ks[7], (DEPTH, CONV_WIDTH, D_RNN), CONV_WIDTH ** -0.5),
        "conv_b": nrm(ks[8], (DEPTH, D_RNN), 0.02),
        "w_rec_gate": nrm(ks[9], (DEPTH, RNN_BLOCKS, RNN_BLOCK, RNN_BLOCK), RNN_BLOCK ** -0.5),
        "b_rec_gate": nrm(ks[10], (DEPTH, D_RNN), 0.02),
        "w_in_gate": nrm(ks[11], (DEPTH, RNN_BLOCKS, RNN_BLOCK, RNN_BLOCK), RNN_BLOCK ** -0.5),
        "b_in_gate": nrm(ks[13], (DEPTH, D_RNN), 0.02),
        "lru_lambda": lru_lambda,
        "w_out": nrm(ks[14], (DEPTH, D_MIX, D_MODEL), D_MIX ** -0.5),
        "ffn_norm": gain(ks[15], (DEPTH, D_MODEL)),
        "w_router_group": nrm(ks[16], (DEPTH, D_MODEL, N_GROUPS), D_MODEL ** -0.5),
        "w_router_expert": nrm(ks[17], (DEPTH, D_MODEL, N_EXPERTS), D_MODEL ** -0.5),
        "w_expert_gate": nrm(ks[18], (DEPTH, N_EXPERTS, D_MODEL, D_EXPERT), D_MODEL ** -0.5),
        "w_expert_up": nrm(ks[19], (DEPTH, N_EXPERTS, D_MODEL, D_EXPERT), D_MODEL ** -0.5),
        "w_expert_down": nrm(ks[20], (DEPTH, N_EXPERTS, D_EXPERT, D_MODEL), D_EXPERT ** -0.5),
        "ple_norm": gain(ks[21], (DEPTH, D_MODEL)),
        "w_ple_gate": nrm(ks[22], (DEPTH, D_MODEL, D_MODEL), D_MODEL ** -0.5),
        "w_ple_up": nrm(ks[23], (DEPTH, D_PLE, D_MODEL), D_PLE ** -0.5),
    }

def second_block(x, p, mix_norm, w_in, b_forget, q_norm, k_norm, conv_w, conv_b,
              w_rec_gate, b_rec_gate, w_in_gate, b_in_gate, lru_lambda, w_out,
              ffn_norm, w_router_group, w_router_expert, w_expert_gate,
              w_expert_up, w_expert_down, ple_norm, w_ple_gate, w_ple_up):
    h = x
    b, s, _ = x.shape
    for i in range(DEPTH):
        hn = rms_norm(h, mix_norm[i])
        proj = hn @ w_in[i]
        q = rms_norm(proj[..., COL_Q:COL_K].reshape(b, s, ATT_HEADS, HEAD_DIM), q_norm[i])
        k = rms_norm(proj[..., COL_K:COL_V].reshape(b, s, ATT_HEADS, HEAD_DIM), k_norm[i])
        v = proj[..., COL_V:COL_F].reshape(b, s, ATT_HEADS, HEAD_DIM)
        log_f = jax.nn.log_sigmoid((proj[..., COL_F:COL_RX] + b_forget[i]).astype(jnp.float32))
        att_out = forgetting_attention(q, k, v, log_f)

        rx = causal_depthwise_conv(proj[..., COL_RX:COL_RG], conv_w[i], conv_b[i])
        rnn = rg_lru(rx, w_rec_gate[i], b_rec_gate[i], w_in_gate[i], b_in_gate[i], lru_lambda[i])
        rnn_out = jax.nn.gelu(proj[..., COL_RG:D_IN_PROJ], approximate=True) * rnn

        h = h + jnp.concatenate([att_out, rnn_out], axis=-1) @ w_out[i]

        hn = rms_norm(h, ffn_norm[i])
        h = h + hierarchical_moe(hn, w_router_group[i], w_router_expert[i],
                                 w_expert_gate[i], w_expert_up[i], w_expert_down[i])

        gate = jax.nn.sigmoid(rms_norm(h, ple_norm[i]) @ w_ple_gate[i])
        h = h + gate * (p[i] @ w_ple_up[i])
    return h


def setup_inputs(seed=0):
    out = dict(first_inputs(seed))
    for name, value in second_inputs(seed + 1).items():
        if name != "x":
            out[name + "_2"] = value
    return out


def reference(
    x, attn_norm, w_in, attn_sinks, w_attn_branch, w_ret_branch, w_out, ffn_norm, w_peer_query,
    peer_sub_keys, peer_expert_down, peer_expert_up, final_norm, p_2, mix_norm_2, w_in_2,
    b_forget_2, q_norm_2, k_norm_2, conv_w_2, conv_b_2, w_rec_gate_2, b_rec_gate_2, w_in_gate_2,
    b_in_gate_2, lru_lambda_2, w_out_2, ffn_norm_2, w_router_group_2, w_router_expert_2,
    w_expert_gate_2, w_expert_up_2, w_expert_down_2, ple_norm_2, w_ple_gate_2, w_ple_up_2,
):
    x = first_block(
        x, attn_norm, w_in, attn_sinks, w_attn_branch, w_ret_branch, w_out, ffn_norm,
        w_peer_query, peer_sub_keys, peer_expert_down, peer_expert_up, final_norm,
    )
    return second_block(
        x, p_2, mix_norm_2, w_in_2, b_forget_2, q_norm_2, k_norm_2, conv_w_2, conv_b_2,
        w_rec_gate_2, b_rec_gate_2, w_in_gate_2, b_in_gate_2, lru_lambda_2, w_out_2, ffn_norm_2,
        w_router_group_2, w_router_expert_2, w_expert_gate_2, w_expert_up_2, w_expert_down_2,
        ple_norm_2, w_ple_gate_2, w_ple_up_2,
    )


_drawn_inputs = setup_inputs


def setup_inputs(seed=0):
    import zlib

    import numpy as np

    out = dict(_drawn_inputs(seed))
    spreads = {}
    factors = {'attn_sinks': 3.276,
     'mix_norm_2': 3.021,
     'b_forget_2': 3.424,
     'q_norm_2': 8.0,
     'k_norm_2': 4.865,
     'b_rec_gate_2': 21.521,
     'b_in_gate_2': 8.0,
     'ple_norm_2': 64.0,
     'ffn_norm_2': 6.499}
    for name, (base, spread) in spreads.items():
        noise = np.random.default_rng([zlib.crc32(name.encode()), seed]).standard_normal(out[name].shape)
        drawn = base * np.exp(spread * noise) if base else spread * noise
        out[name] = __import__('jax').numpy.asarray(drawn.astype(out[name].dtype))
    for name, factor in factors.items():
        out[name] = (out[name] * factor).astype(out[name].dtype)
    return out
```

```python
import concourse.bass as bass
from concourse import mybir
from contextlib import ExitStack

P = 128
D = 2048
T2 = 2
KC = D // P
CH = 512
SLOTS = 4
UNIT = 4096
HEADS = 8
HD = 128
EXPERTS = 32
DE = 256
TOPK = 16
EPS = 1e-6
NEG = -1e30
LOWEST = -3e38

QA, KA, VA, QR, KR, VR, GR, P1W = 0, 1024, 1280, 1536, 2560, 3584, 5632, 7680
GATE_A, GATE_R = P1W, P1W + D
Q2, K2, V2, RN2, P2W = 0, 1024, 2048, 3072, 4096
W2_F, W2_RX, W2_RG = 3072, 3080, 4104

UA, UB, UC, UD, UE, UF, UG, UH = 0, 30, 58, 66, 74, 94, 102, 198
QCA, QCB, QCC, QCD, QCE, QCF, QCH = 0, 15, 23, 27, 31, 41, 45
CREDITS = 4

CONST_AT = {}
CONST_W = 0
for _name, _width in (("ident", 128), ("cos", 128), ("sin", 128), ("wmask", 256), ("cmask", 256),
                      ("decay", 1024), ("qdecay", 8), ("kdecay", 8), ("tri", 256), ("sel", 1024),
                      ("iota16", 16), ("iota32", 32), ("eps", 1)):
    CONST_AT[_name] = (CONST_W, CONST_W + _width)
    CONST_W += _width
CHUNK_E = [("rx", 0), ("rx", 1), ("q", 0), ("q", 1), ("k", 0), ("k", 1), ("v", 0), ("v", 1),
           ("rg", 0), ("rg", 1)]


def steps_of_first_block():
    after = {6: [("tr", QA, QA, 512)], 7: [("tr", QA + 512, QA + 512, 512)], 8: [("tr", KA, KA, 256)],
             9: [("S", 0)], 10: [("T", 0), ("V", 0), ("S", 1)], 11: [("T", 1), ("V", 1), ("S", 2)],
             12: [("T", 2), ("V", 2), ("S", 3)], 13: [("T", 3), ("V", 3)],
             15: [("tr", QR, QR, 512)], 16: [("tr", QR + 512, QR + 512, 512)],
             17: [("tr", KR, KR, 512)], 18: [("tr", KR + 512, KR + 512, 512)],
             3: [("rope", 0)], 5: [("rope", 1)], 14: [("rope", 2), ("rope", 3)],
             30: [("R", 8), ("rnorm", 0)],
             33: [("tr", GR + 512 * j, QR + 512 * j, 512) for j in range(4)]}
    for i in range(8):
        after[22 + i] = [("R", i)]
    for n in range(4):
        after.setdefault(UB + 7 * n + 1, []).append(("gate", n, 0))
        after.setdefault(UB + 7 * n + 3, []).append(("gate", n, 1))
        after[UB + 7 * n + 6] = [("merge", n)]
        if n:
            after[UB + 7 * n + 2] = [("tr", VR + 512 * (n - 1), GR + 512 * (n - 1), 512)]
    after[UB + 27].append(("tr", VR + 1536, GR + 1536, 512))
    return after


def steps_of_second_block():
    return {1: [("FL", 0)], 3: [("conv", 0)], 4: [("LG", 0)], 5: [("LG", 1), ("lru", 0)],
            6: [("FC", 0)], 7: [("qknorm", 0)], 9: [("tr", Q2, Q2, 512)],
            10: [("tr", Q2 + 512, Q2 + 512, 512)],
            11: [("qknorm", 1)], 13: [("tr", K2, K2, 512)], 14: [("tr", K2 + 512, K2 + 512, 512)],
            15: [("S", 4)], 16: [("T", 4), ("V", 4), ("S", 5)], 17: [("T", 5), ("V", 5), ("S", 6)],
            18: [("T", 6), ("V", 6), ("S", 7)], 19: [("T", 7), ("V", 7), ("gelu", 0)]}


def two_blocks(nc, A, consts, out):
    f32, u32 = mybir.dt.float32, mybir.dt.uint32
    ALU, ACT, AX = mybir.AluOpType, mybir.ActivationFunctionType, mybir.AxisListType.X
    AFTER1, AFTER2 = steps_of_first_block(), steps_of_second_block()
    ds = bass.ds

    ctx = ExitStack()
    with ctx:
        def sb(name, shape, dt=f32):
            return ctx.enter_context(nc.sbuf_tensor(name, shape, dt))

        def sem(name):
            return ctx.enter_context(nc.semaphore(name))

        H = sb("H", [P, T2, D])
        XT = sb("XT", [P, T2, D])
        XS = sb("XS", [P, T2, D])
        W = sb("W", [P, SLOTS, UNIT])
        big = sb("big", [P, 19456])
        C = sb("C", [P, CONST_W])
        gains_raw = big[:, 0:256].rearrange("p (a n) -> p a n", a=2)
        GT = sb("GT", [P, 144])
        WR = sb("WR", [P, KC, 36])
        WF = sb("WF", [P, KC, 8])
        rowc = sb("rowc", [P, 272])
        small = sb("small", [P, 640])
        idx_all = big[:, 4608:4864].bitcast(u32).rearrange("p (t n) -> p t n", t=2)
        gate_all = big[:, 4864:5120].rearrange("p (t n) -> p t n", t=2)
        idx_cur = sb("idx_cur", [P, 2, TOPK], u32)

        def const(name):
            return C[:, CONST_AT[name][0]:CONST_AT[name][1]]

        ident = const("ident")
        eps = const("eps")
        cos = const("cos").rearrange("p (t d) -> p t d", t=2)
        sin = const("sin").rearrange("p (t d) -> p t d", t=2)
        XSf = XS[:, :, :].rearrange("p t n -> p (t n)")
        sinks, b_forget = rowc[:, 0:8], rowc[:, 8:16]
        qk_gain = [rowc[:, 16:144], rowc[:, 144:272]]
        conv_w = GT[:, 80:112].rearrange("p (k n) -> p k n", k=4)
        conv_b, b_rec, b_ing, lam = (GT[:, 112 + 8 * j:120 + 8 * j] for j in range(4))

        P1 = big[:, 0:2 * P1W].rearrange("p (t n) -> p t n", t=2)
        KDEC = big[:, 15360:16384].rearrange("p (h d) -> p h d", h=8)
        IN = big[:, 18432:18944].rearrange("p (b t c) -> p b t c", b=2, t=2)
        KV = big[:, 18944:19456].rearrange("p (b e) -> p b e", b=2)
        QT = big[:, 0:4096].rearrange("p (t n) -> p t n", t=2)
        KT = big[:, 4096:6144].rearrange("p (b n) -> p b n", b=16)
        KEYS = big[:, 6144:8192].rearrange("p (b d) -> p b d", b=16)
        S = big[:, 8192:12288].rearrange("p (t b n) -> p t b n", t=2, b=16)
        HN = big[:, 12288:16384].rearrange("p (t n) -> p t n", t=2)
        GROW = big[:, 16384:18432]
        CAND = big[:, 0:2048].rearrange("p (h c) -> p h c", h=8)
        HOT = big[:, 2048:4096].rearrange("p (h b i) -> p h b i", h=8, b=16)
        PU = big[:, 4096:4608].bitcast(u32).rearrange("p (a h b) -> p a h b", a=4, h=8)
        TV = big[:, 6144:6656].rearrange("p (t h q k) -> p t h q k", t=2, h=8, q=2)
        TIU = big[:, 6656:7168].bitcast(u32).rearrange("p (t h q k) -> p t h q k", t=2, h=8, q=2)
        TIF = big[:, 7168:7680].rearrange("p (t h q k) -> p t h q k", t=2, h=8, q=2)
        BV = big[:, 7680:7936].rearrange("p (t h k) -> p t h k", t=2, h=8)
        PF = big[:, 18432:18944].rearrange("p (a h b) -> p a h b", a=4, h=8)
        P2 = big[:, 0:2 * P2W].rearrange("p (t n) -> p t n", t=2)
        RXP = 260
        RX = big[:, 8192:8192 + 8 * RXP].rearrange("p (b s) -> p b s", b=8)
        DECAY_A = RX[:, :, 0:256]
        WREC = big[:, 10272:11296].rearrange("p (b j) -> p b j", b=8)
        WING = big[:, 11296:12320].rearrange("p (b j) -> p b j", b=8)
        TMP = big[:, 10272:12320].rearrange("p (b s) -> p b s", b=8)
        RGATE = big[:, 12320:14368].rearrange("p (b s) -> p b s", b=8)
        IGATE = big[:, 14368:16416].rearrange("p (b s) -> p b s", b=8)
        XC = XSf[:, 0:2048].rearrange("p (b s) -> p b s", b=8)
        GELU = XSf[:, 2048:4096].rearrange("p (b s) -> p b s", b=8)
        PX = P2[:, :, RN2:P2W]
        CT = small[:, 384:640]
        SM = big[:, 16416:17440].rearrange("p (h k) -> p h k", h=4)
        PT = big[:, 17440:18464].rearrange("p (t c) -> p t c", t=2)
        PT1 = big[:, 17408:18432].rearrange("p (t c) -> p t c", t=2)
        SM1 = big[:, 16384:17408].rearrange("p (h k) -> p h k", h=4)
        HID = big[:, 0:1024].rearrange("p (b f s) -> p b f s", b=2, f=2)
        PIN = big[:, 1024:1536].rearrange("p (t n) -> p t n", t=2)
        PINT = big[:, 1536:2048].rearrange("p (t n) -> p t n", t=2)
        WUP = big[:, 2048:6144].rearrange("p (k n) -> p k n", k=2)

        ss, rms, rstd = small[:, 0:2], small[:, 2:4], small[:, 4:6]
        mx, nmx, rs, es, rden = (small[:, 8 + 4 * j:12 + 4 * j] for j in range(5))
        STATS = small[:, 32:128].rearrange("p (g s) -> p g s", g=16)
        MV = small[:, 128:160].rearrange("p (g s) -> p g s", g=16)
        ORMS, ORSTD = small[:, 160:176], small[:, 176:192]
        hrms = small[:, 192:208].rearrange("p (t h) -> p t h", t=2)
        hrstd = small[:, 208:224].rearrange("p (t h) -> p t h", t=2)
        SPV = small[:, 224:248]
        SPZ, SPS, SPQ, SPA = (small[:, 248 + 24 * j:272 + 24 * j] for j in range(4))
        CUM = small[:, 344:360].rearrange("p (t h) -> p t h", t=2)
        LF = small[:, 360:376].rearrange("p (t h) -> p t h", t=2)
        lru_neg, lru_pos = small[:, 376:384], small[:, 0:8]
        dots = small[:, 32:48]
        acts = small[:, 48:64]
        wts = small[:, 64:80]
        COMB = small[:, 384:448].rearrange("p (t e) -> p t e", t=2)
        RL = small[:, 32:112].rearrange("p (t e) -> p t e", t=2)
        ML = small[:, 112:176].rearrange("p (t e) -> p t e", t=2)
        TOPV = small[:, 176:208].rearrange("p (t g e) -> p t g e", t=2, g=2)
        TOPU = small[:, 208:240].bitcast(u32).rearrange("p (t g e) -> p t g e", t=2, g=2)
        TOPF = small[:, 240:272].rearrange("p (t g e) -> p t g e", t=2, g=2)
        GEXP = small[:, 272:280].rearrange("p (t g) -> p t g", t=2)
        RSC = small[:, 280:296].rearrange("p (t g) -> p t g", t=2)
        HOT32 = small[:, 448:512].rearrange("p (t e) -> p t e", t=2)

        bank = [ctx.enter_context(nc.psum_tensor(f"bank{i}", [P, CH], f32)) for i in range(8)]

        w_loaded = [sem(f"w_loaded{s}") for s in range(SLOTS)]
        w_used = sem("w_used")
        set_free = sem("set_free")
        x_loaded, c_loaded, g_loaded = sem("x_loaded"), sem("c_loaded"), sem("g_loaded")
        gt_turned, gt_ready = sem("gt_turned"), sem("gt_ready")
        rms_ready, xs_ready, x_turned = sem("rms_ready"), sem("xs_ready"), sem("x_turned")
        xt_act, xt_dve = sem("xt_act"), sem("xt_dve")
        roped = sem("roped")
        turned, turn_kept = sem("turned"), sem("turn_kept")
        scored, scores_ready, exp_ready, probs_ready = (
            sem(n) for n in ("scored", "scores_ready", "exp_ready", "probs_ready"))
        probs_turned, probs_kept, attended, attn_kept = (
            sem(n) for n in ("probs_turned", "probs_kept", "attended", "attn_kept"))
        ret_inner, inner_ready, state_ready, ret_out, ret_stats, ret_kept = (
            sem(n) for n in ("ret_inner", "inner_ready", "state_ready", "ret_out", "ret_stats", "ret_kept"))
        var_ready, ret_rms, ret_ready = sem("var_ready"), sem("ret_rms"), sem("ret_ready")
        merged = sem("merged")
        keys_loaded, grow_loaded, hn_ready = sem("keys_loaded"), sem("grow_loaded"), sem("hn_ready")
        keys_turned, keys_kept, peer_scored, s_kept = (
            sem(n) for n in ("keys_turned", "keys_kept", "peer_scored", "s_kept"))
        best_ready, gate_exp, idx_ready = sem("best_ready"), sem("gate_exp"), sem("idx_ready")
        down_in = [sem(f"down_in{b}") for b in range(4)]
        up_in = [sem(f"up_in{b}") for b in range(4)]
        gathers = sem("gathers")
        dotted, weight_ready, added = sem("dotted"), sem("weight_ready"), sem("added")
        peer_done, fin_rms, x2_ready = sem("peer_done"), sem("fin_rms"), sem("x2_ready")
        lru_loaded = sem("lru_loaded")
        fl_done, sp_in, sp_exp, sp_done, cum_done, cum_kept = (
            sem(n) for n in ("fl_done", "sp_in", "sp_exp", "sp_done", "cum_done", "cum_kept"))
        conv_ready, lru_mm, gates_ready, decay_ready, gap_ready, gap_root, state_rnn, rnn_ready = (
            sem(n) for n in ("conv_ready", "lru_mm", "gates_ready", "decay_ready", "gap_ready",
                             "gap_root", "state_rnn", "rnn_ready"))
        hsq_ready, hrms_ready, qk_ready = sem("hsq_ready"), sem("hrms_ready"), sem("qk_ready")
        routed, route_in, route_exp, comb_ready = (
            sem(n) for n in ("routed", "route_in", "route_exp", "comb_ready"))
        gate_up, silu_ready, hid_ready, down_done, moe_added = (
            sem(n) for n in ("gate_up", "silu_ready", "hid_ready", "down_done", "moe_added"))
        ple_loaded, up_done, out_ready, out_stored = (
            sem(n) for n in ("ple_loaded", "up_done", "out_ready", "out_stored"))

        block = ctx.enter_context(nc.Block())

        def unit_count(u):
            return 16 * (u // SLOTS + 1)

        def slot(u, n):
            return W[:, u % SLOTS, :].rearrange("p (k n) -> p k n", n=n)

        def group(n):
            return 4 * ((n // 2) % 2), n % 2, P * (n % 2 + 1)

        def att(n):
            return (P1, QA, KA, VA, SM1, PT1) if n < 4 else (P2, Q2, K2, V2, SM, PT)

        @block.sync
        def _(sp):
            def load(u, src, i=None, per=0, n=CH):
                more = 0 if i is None else i * per
                if u >= SLOTS:
                    sp.wait_ge(w_used, more + (u - SLOTS + 1) if i is not None else u - SLOTS + 1)
                sp.dma_start(slot(u, n), src).then_inc(w_loaded[u % SLOTS], 16)

            def rows(w, k0, k, c, n=CH):
                return w.rearrange("(k p) n -> p k n", p=P)[:, k0:k0 + k, ds(c, n)]

            w_in, w_ab, w_rb, w_out = A["w_in"][0], A["w_attn_branch"][0], A["w_ret_branch"][0], A["w_out"][0]
            sp.dma_start(H[:, :, :], A["x"][0].rearrange("(t p) n -> p t n", p=P)).then_inc(x_loaded, 16)
            sp.dma_start(C[:, :], consts).then_inc(c_loaded, 16)
            for u in range(4):
                load(u, rows(w_in, 8 * (u % 2), 8, CH * (u // 2)))
            with sp.Fori(0, 6) as i:
                for j in range(4):
                    load(UA + 4 + j, rows(w_in, 8 * (j % 2), 8, i * (2 * CH) + (2 + j // 2) * CH), i, 4)
            for u in (28, 29):
                load(u, rows(w_in, 8 * (u % 2), 8, CH * 14))
            for n in range(4):
                u = UB + 7 * n
                for j in range(2):
                    load(u + j, rows(w_in, 8 * j, 8, GATE_A + CH * n))
                for j in range(2):
                    load(u + 2 + j, rows(w_in, 8 * j, 8, GATE_R + CH * n))
                load(u + 4, rows(w_ab, 0, 8, CH * n))
                for j in range(2):
                    load(u + 5 + j, rows(w_rb, 8 * j, 8, CH * n))

            def load_square(u0, w):
                with sp.Fori(0, 2) as i:
                    for j in range(4):
                        load(u0 + j, rows(w, 8 * (j % 2), 8, i * (2 * CH) + (j // 2) * CH), i, 4)

            load_square(UC, w_out)
            load_square(UD, A["w_peer_query"][0])
            sp.wait_ge(w_used, UD)
            sp.dma_start(KEYS, A["peer_sub_keys"][0].rearrange("q h n d -> n (q h) d")).then_inc(keys_loaded, 16)
            sp.dma_start(GROW, A["ffn_norm"].to_broadcast([P, D])).then_inc(grow_loaded, 16)
            sp.wait_ge(hn_ready, 2)
            sp.dma_start(GROW, A["final_norm"].unsqueeze(0).to_broadcast([P, D])).then_inc(grow_loaded, 16)
            sp.wait_ge(peer_done, 1)
            w2 = A["w_in_2"][0]
            col = {"q": Q2, "k": K2, "v": V2, "rx": W2_RX, "rg": W2_RG}
            sp.dma_start(WREC, A["w_rec_gate_2"][0].rearrange("b i j -> i b j")).then_inc(lru_loaded, 16)
            sp.dma_start(WING, A["w_in_gate_2"][0].rearrange("b i j -> i b j")).then_inc(lru_loaded, 16)
            for c, (kind, n) in enumerate(CHUNK_E):
                for j in range(2):
                    load(UE + 2 * c + j, rows(w2, 8 * j, 8, col[kind] + CH * n))
            load_square(UF, A["w_out_2"][0])
            sp.wait_ge(w_used, UG)
            sp.dma_start(PIN, A["p_2"][0, 0].rearrange("(t p) n -> p t n", p=P)).then_inc(ple_loaded, 16)
            sp.dma_start(WUP, A["w_ple_up_2"][0].rearrange("(k p) n -> p k n", p=P)).then_inc(ple_loaded, 16)
            wg = A["w_expert_gate_2"].rearrange("o e (k p) n -> p (o e k) n", p=P)
            wu = A["w_expert_up_2"].rearrange("o e (k p) n -> p (o e k) n", p=P)
            wd = A["w_expert_down_2"].rearrange("o e (k p) n -> p (o e k) n", p=P)
            with sp.Fori(0, EXPERTS // 4) as i:
                for e in range(4):
                    load(UG + 3 * e, wg[:, ds(i * (4 * KC) + e * KC, KC), :], i, 12, DE)
                    load(UG + 3 * e + 1, wu[:, ds(i * (4 * KC) + e * KC, KC), :], i, 12, DE)
                    load(UG + 3 * e + 2, wd[:, ds(i * 8 + e * 2, 2), :], i, 12, D)
            load_square(UH, A["w_ple_gate_2"][0])
            out_t = out[0].rearrange("(t p) n -> p t n", p=P)
            for n in range(4):
                sp.wait_ge(out_ready, n + 1)
                sp.dma_start(out_t[:, :, CH * n:CH * (n + 1)], H[:, :, CH * n:CH * (n + 1)]).then_inc(out_stored, 16)
            sp.wait_ge(out_stored, 64)

        @block.gpsimd
        def _(pool):
            r = 0
            for name in ("attn_norm", "ffn_norm", "mix_norm_2", "ffn_norm_2", "ple_norm_2"):
                pool.dma_start(gains_raw[r:r + 16, 0, :], A[name].rearrange("o (k p) -> (o k) p", p=P)).then_inc(g_loaded, 16)
                r += 16
            pool.dma_start(gains_raw[0:32, 1, :], A["conv_w_2"].rearrange("o c (k p) -> (o c k) p", p=P)).then_inc(g_loaded, 16)
            r = 32
            for name in ("conv_b_2", "b_rec_gate_2", "b_in_gate_2", "lru_lambda_2"):
                pool.dma_start(gains_raw[r:r + 8, 1, :], A[name].rearrange("o (k p) -> (o k) p", p=P)).then_inc(g_loaded, 16)
                r += 8
            pool.dma_start(rowc[:, 0:8], A["attn_sinks"].to_broadcast([P, 8])).then_inc(g_loaded, 16)
            pool.dma_start(rowc[:, 8:16], A["b_forget_2"].to_broadcast([P, 8])).then_inc(g_loaded, 16)
            pool.dma_start(rowc[:, 16:144], A["q_norm_2"].to_broadcast([P, P])).then_inc(g_loaded, 16)
            pool.dma_start(rowc[:, 144:272], A["k_norm_2"].to_broadcast([P, P])).then_inc(g_loaded, 16)
            pool.dma_start(WR[:, :, 0:4], A["w_router_group_2"][0].rearrange("(k p) n -> p k n", p=P)).then_inc(g_loaded, 16)
            pool.dma_start(WR[:, :, 4:36], A["w_router_expert_2"][0].rearrange("(k p) n -> p k n", p=P)).then_inc(g_loaded, 16)
            pool.dma_start(WF[:, :, :], A["w_in_2"][0].rearrange("(k p) n -> p k n", p=P)[:, :, W2_F:W2_F + 8]).then_inc(g_loaded, 16)
            down_t, up_t = A["peer_expert_down"][0], A["peer_expert_up"][0]
            pool.wait_ge(w_used, UE)
            for t in range(T2):
                pool.wait_ge(idx_ready, t + 1)
                with pool.Fori(0, HEADS // 2) as i:
                    for j in range(2 * TOPK):
                        idx = idx_cur[:, j // TOPK, :]
                        at = TOPK * HEADS * t + j
                        if j % TOPK == 0:
                            pool.tensor_copy(idx, idx_all[:, t, ds(i * (2 * TOPK) + j, TOPK)])
                            pool.drain()
                        row = bass.IndirectOffsetOnAxis(idx[:, j % TOPK:j % TOPK + 1], 0)
                        pool.wait_ge(dotted, i * (2 * TOPK) + (at + 1))
                        pool.sem_inc(gathers, 1)
                        pool.indirect_dma_start(W[:, j % 4 // 2, (j % 2) * D:(j % 2 + 1) * D],
                                                None, down_t, row).then_inc(down_in[j % 4], 16)
                        pool.wait_ge(added, i * (2 * TOPK) + (at + 1))
                        pool.sem_inc(gathers, 1)
                        pool.indirect_dma_start(W[:, 2 + j % 4 // 2, (j % 2) * D:(j % 2 + 1) * D],
                                                None, up_t, row).then_inc(up_in[j % 4], 16)

        @block.tensor
        def _(pe):
            turns = 0

            def xt(k, t):
                return XT[:, t, k * P:(k + 1) * P]

            def turn_norm(j):
                pe.wait_ge(xs_ready, 2 * (j + 1))
                for k in range(KC):
                    if k >= 4:
                        pe.wait_ge(xt_dve if k % 2 else xt_act, 8 * j + (k - 4) // 2 + 1)
                    for t in range(T2):
                        last = pe.transpose(bank[4 + k % 4][:, t * P:(t + 1) * P], XS[:, t, k * P:(k + 1) * P], ident)
                    last.then_inc(x_turned, 1)
                pe.wait_ge(xt_act, 8 * (j + 1))
                pe.wait_ge(xt_dve, 8 * (j + 1))

            def wait_unit(u, i=None, per=0):
                more = 0 if i is None else i * (16 * per // SLOTS)
                pe.wait_ge(w_loaded[u % SLOTS], more + unit_count(u) if i is not None else unit_count(u))

            def wait_set(q, i=None):
                pe.wait_ge(set_free, i * 4 + (2 * q + 2) if i is not None else 2 * q + 2)

            def unit_natural(u, ps, lhs, k0, kn, first, last_unit, i=None, per=0):
                wait_unit(u, i, per)
                w = slot(u, CH)
                for t in range(T2):
                    for k in range(kn):
                        mm = pe.matmul(ps[t][:, :], lhs(k0 + k, t), w[:, k, :],
                                       start=first and k == 0, stop=last_unit and k == kn - 1)
                mm.then_inc(w_used, 1)

            def chunk_turned(u, ps, i=None, per=0):
                wait_unit(u, i, per)
                wait_unit(u + 1, i, per)
                for b in range(4):
                    o = ps[b // 2][:, (b % 2) * 256:(b % 2 + 1) * 256].rearrange("p (t s) -> p t s", t=2)
                    for k in range(KC):
                        mm = pe.matmul(o, slot(u + k // 8, CH)[:, k % 8, b * P:(b + 1) * P],
                                       XT[:, :, k * P:(k + 1) * P], start=k == 0, stop=k == KC - 1)
                mm.then_inc(w_used, 2)

            def square(u0, q0, lhs):
                with pe.Fori(0, 2) as i:
                    for c in range(2):
                        q, u = q0 + c, u0 + 2 * c
                        wait_set(q, i)
                        ps = bank[2 * (q % 2):2 * (q % 2) + 2]
                        for j in range(2):
                            unit_natural(u + j, ps, lhs, 8 * j, 8, j == 0, j == 1, i, 4)

            def turn(buf, src, n):
                nonlocal turns
                pe.wait_ge(attn_kept, scored_so_far) if scored_so_far else None
                for c in range(0, n, 256):
                    if turns >= 4:
                        pe.wait_ge(turn_kept, turns - 3)
                    for t in range(T2):
                        for b in range(2):
                            at = src + c + b * P
                            last = pe.transpose(bank[4 + turns % 4][:, (2 * t + b) * P:(2 * t + b + 1) * P],
                                                buf[:, t, at:at + P], ident)
                    last.then_inc(turned, 1)
                    turns += 1

            scored_so_far = 0

            def scores(n):
                nonlocal scored_so_far
                buf, cq, ck, _, _, _ = att(n)
                h0, t, nk = group(n)
                pe.wait_ge(turn_kept, turns)
                if n:
                    pe.wait_ge(attn_kept, n)
                if n >= 4:
                    pe.wait_ge(cum_kept, 2)
                for hh in range(4):
                    h = h0 + hh
                    o = bank[4 + hh // 2][:, (hh % 2) * 256:(hh % 2) * 256 + nk]
                    kcol = ck + (h0 // 4 * P if n < 4 else h * P)
                    keys = buf[:, 0:2, kcol:kcol + P] if nk > P else buf[:, 0, kcol:kcol + P]
                    mm = pe.matmul(o.rearrange("p (t s) -> p t s", s=P) if nk > P else o,
                                   buf[:, t, cq + h * P:cq + (h + 1) * P], keys, start=True, stop=n < 4)
                    if n >= 4:
                        mm = pe.matmul(o, const("sel")[:, h * P:(h + 1) * P], CT[:, 0:nk], start=False, stop=True)
                mm.then_inc(scored, 1)
                scored_so_far = n + 1

            def turn_probs(n):
                _, _, _, _, sm, _ = att(n)
                h0, t, nk = group(n)
                pe.wait_ge(probs_ready, n + 1)
                for kt in range(nk // P):
                    for hh in range(4):
                        last = pe.transpose(bank[6 + kt][:, hh * P:(hh + 1) * P], sm[:, hh, kt * P:(kt + 1) * P], ident)
                last.then_inc(probs_turned, 1)

            def values(n):
                buf, _, _, cv, _, pt = att(n)
                h0, t, nk = group(n)
                pe.wait_ge(probs_kept, n + 1)
                nt = nk // P
                if n < 4:
                    v = cv + h0 // 4 * P
                    for kt in range(nt):
                        mm = pe.matmul(bank[4][:, :], buf[:, kt, v:v + P], pt[:, kt, :], start=kt == 0, stop=kt == nt - 1)
                else:
                    for hh in range(4):
                        v = cv + (h0 + hh) * P
                        for kt in range(nt):
                            mm = pe.matmul(bank[4][:, hh * P:(hh + 1) * P], buf[:, kt, v:v + P],
                                           pt[:, kt, hh * P:(hh + 1) * P], start=kt == 0, stop=kt == nt - 1)
                mm.then_inc(attended, 1)

            def retention(i):
                if i == 0:
                    pe.wait_ge(turn_kept, turns)
                    pe.wait_ge(attn_kept, 4)
                if i < HEADS:
                    if i:
                        pe.wait_ge(inner_ready, i)
                        pe.wait_ge(state_ready, i)
                    for t in range(T2):
                        mm = pe.matmul(bank[4][:, t * P:(t + 1) * P], P1[:, t, KR + i * P:KR + (i + 1) * P],
                                       P1[:, t, QR + i * P:QR + (i + 1) * P], start=True, stop=True)
                    mm = pe.matmul(bank[5][:, 0:256], KDEC[:, i, :], P1[:, 0, VR + 256 * i:VR + 256 * (i + 1)],
                                   start=True, stop=True)
                    mm.then_inc(ret_inner, 1)
                if i:
                    h = i - 1
                    pe.wait_ge(inner_ready, h + 1)
                    pe.wait_ge(state_ready, h + 1)
                    if h >= 2:
                        pe.wait_ge(ret_stats, h - 1)
                        pe.wait_ge(ret_kept, h - 1)
                    o = bank[6 + h % 2]
                    v = VR + 256 * h
                    pe.matmul(o[:, 0:256], IN[:, h % 2, 0, :], P1[:, 0, v:v + 256], start=True, stop=True)
                    pe.matmul(o[:, 256:512], IN[:, h % 2, 1, :], P1[:, 1, v:v + 256], start=True, stop=False)
                    pe.matmul(o[:, 256:512], P1[:, 1, QR + h * P:QR + (h + 1) * P], KV[:, h % 2, :],
                              start=False, stop=True).then_inc(ret_out, 1)

            pe.wait_ge(c_loaded, 16)
            pe.wait_ge(g_loaded, 17 * 16)
            pe.transpose(bank[4][:, 0:80], gains_raw[0:80, 0, :], ident[0:80, 0:80])
            pe.transpose(bank[5][:, 0:64], gains_raw[0:64, 1, :], ident[0:64, 0:64]).then_inc(gt_turned, 1)
            pe.wait_ge(gt_ready, 2)
            turn_norm(0)

            ready = {QA: (roped, 1), QA + 512: (roped, 1), KA: (roped, 2), QR: (roped, 3), QR + 512: (roped, 3),
                     KR: (roped, 4), KR + 512: (roped, 4), **{GR + 512 * j: (ret_ready, 1) for j in range(4)},
                     **{VR + 512 * j: (merged, j + 1) for j in range(4)}}
            for u in range(UB + 28):
                if u < UB:
                    if u % 2 == 0:
                        wait_set(u // 2)
                    q = u // 2
                    unit_natural(u, bank[2 * (q % 2):2 * (q % 2) + 2], xt, 8 * (u % 2), 8, u % 2 == 0, u % 2 == 1)
                else:
                    n, j = (u - UB) // 7, (u - UB) % 7
                    if j < 4:
                        q = QCB + 2 * n + j // 2
                        if j % 2 == 0:
                            wait_set(q)
                        unit_natural(u, bank[2 * (q % 2):2 * (q % 2) + 2], xt, 8 * (j % 2), 8, j % 2 == 0, j % 2 == 1)
                    elif j == 4:
                        pe.wait_ge(turn_kept, turns)
                        pe.wait_ge(ret_stats, HEADS)
                        pe.wait_ge(ret_kept, HEADS)
                        if n:
                            pe.wait_ge(merged, n)
                        unit_natural(u, bank[4:6], lambda k, t: P1[:, t, QA + k * P:QA + (k + 1) * P], 0, 8, True, True)
                    else:
                        unit_natural(u, bank[6:8], lambda k, t: P1[:, t, QR + k * P:QR + (k + 1) * P],
                                     8 * (j - 5), 8, j == 5, j == 6)
                for step in AFTER1.get(u, ()):
                    if step[0] == "tr":
                        pe.wait_ge(*ready[step[1]])
                        turn(P1, step[1], step[3])
                    elif step[0] == "S":
                        scores(step[1])
                    elif step[0] == "T":
                        turn_probs(step[1])
                    elif step[0] == "V":
                        values(step[1])
                    elif step[0] == "R":
                        retention(step[1])

            pe.wait_ge(turn_kept, turns)
            square(UC, QCC, lambda k, t: P1[:, t, GR + k * P:GR + (k + 1) * P])

            turn_norm(1)
            with pe.Fori(0, 2) as i:
                for c in range(2):
                    q, u = QCD + c, UD + 2 * c
                    wait_set(q, i)
                    chunk_turned(u, bank[2 * (q % 2):2 * (q % 2) + 2], i, 4)
            pe.wait_ge(keys_loaded, 16)
            for b in range(16):
                last = pe.transpose(bank[4 + b // 4][:, (b % 4) * P:(b % 4 + 1) * P], KEYS[:, b, :], ident)
            last.then_inc(keys_turned, 1)
            pe.wait_ge(keys_kept, 4)
            pe.wait_ge(set_free, CREDITS + 2 * (QCD + 4))
            for r in range(8):
                t, b0 = r // 4, 4 * (r % 4)
                if r >= 4:
                    pe.wait_ge(s_kept, r - 3)
                for b in range(b0, b0 + 4):
                    mm = pe.matmul(bank[4 + r % 4][:, (b % 4) * P:(b % 4 + 1) * P], QT[:, t, b * P:(b + 1) * P],
                                   KT[:, (b % 2) * 8 + b // 2, :], start=True, stop=True)
                mm.then_inc(peer_scored, 1)

            turn_norm(2)
            ready2 = {Q2: 1, Q2 + 512: 1, K2: 2, K2 + 512: 2}
            for c, (kind, n) in enumerate(CHUNK_E):
                q = QCE + c
                ps = bank[2 * (q % 2):2 * (q % 2) + 2]
                for half in range(2):
                    u = UE + 2 * c + half
                    if half == 0:
                        wait_set(q)
                    if kind in ("q", "k", "v"):
                        unit_natural(u, ps, xt, 8 * half, 8, half == 0, half == 1)
                    elif half == 1:
                        chunk_turned(u - 1, ps)
                    for step in AFTER2.get(2 * c + half, ()):
                        if step[0] == "tr":
                            pe.wait_ge(qk_ready, ready2[step[1]])
                            turn(P2, step[1], step[3])
                        elif step[0] == "S":
                            scores(step[1])
                        elif step[0] == "T":
                            turn_probs(step[1])
                        elif step[0] == "V":
                            values(step[1])
                        elif step[0] == "FL":
                            for t in range(T2):
                                for k in range(KC):
                                    mm = pe.matmul(bank[4][:, 8 * t:8 * t + 8], xt(k, t), WF[:, k, :],
                                                   start=k == 0, stop=k == KC - 1)
                            mm.then_inc(fl_done, 1)
                        elif step[0] == "LG":
                            if step[1] == 0:
                                pe.wait_ge(conv_ready, 1)
                                pe.wait_ge(lru_loaded, 32)
                                pe.wait_ge(sp_in, 1)
                            else:
                                pe.wait_ge(gates_ready, 8)
                            for b in range(8):
                                mm = pe.matmul(bank[4 + b // 2][:, (b % 2) * 256:(b % 2 + 1) * 256],
                                               (WING if step[1] else WREC)[:, b, :], XC[:, b, :], start=True, stop=True)
                            mm.then_inc(lru_mm, 1)
                        elif step[0] == "FC":
                            pe.wait_ge(sp_done, 1)
                            pe.wait_ge(gates_ready, 16)
                            tri = const("tri")
                            pe.matmul(bank[4][:, 0:8], tri[:, 0:P], LF[:, 0, :], start=True, stop=True)
                            pe.matmul(bank[4][:, 8:16], tri[:, P:2 * P], LF[:, 0, :], start=True, stop=False)
                            pe.matmul(bank[4][:, 8:16], tri[:, 0:P], LF[:, 1, :], start=False, stop=True)
                            pe.matmul(bank[5][0:8, 0:P], LF[:, 0, :], tri[:, 0:P], start=True, stop=True)
                            pe.matmul(bank[5][0:8, P:2 * P], LF[:, 0, :], tri[:, P:2 * P], start=True, stop=False)
                            pe.matmul(bank[5][0:8, P:2 * P], LF[:, 1, :], tri[:, 0:P],
                                      start=False, stop=True).then_inc(cum_done, 1)
            pe.wait_ge(attn_kept, 8)
            pe.wait_ge(rnn_ready, 1)
            square(UF, QCF, lambda k, t: P2[:, t, k * P:(k + 1) * P] if k < 8 else
                   P2[:, t, RN2 + (k - 8) * P:RN2 + (k - 7) * P])

            turn_norm(3)
            for t in range(T2):
                for k in range(KC):
                    mm = pe.matmul(bank[4][:, 64 * t:64 * t + 36], xt(k, t), WR[:, k, :], start=k == 0, stop=k == KC - 1)
            mm.then_inc(routed, 1)
            pe.wait_ge(comb_ready, 1)
            pe.wait_ge(set_free, CREDITS + 2 * QCH)
            with pe.Fori(0, EXPERTS // 4) as i:
                for e in range(4):
                    pe.wait_ge(hid_ready, i * 4 + (e + 1))
                    for j in range(2):
                        u = UG + 3 * e + j
                        wait_unit(u, i, 12)
                        w = slot(u, DE)
                        for f in range(2):
                            o = bank[2 * (e % 2) + j][:, f * 256:(f + 1) * 256].rearrange("p (t s) -> p t s", t=2)
                            for k in range(KC):
                                mm = pe.matmul(o, w[:, k, f * P:(f + 1) * P], XT[:, :, k * P:(k + 1) * P],
                                               start=k == 0, stop=k == KC - 1)
                        mm.then_inc(w_used, 1)
                    u = UG + 3 * e + 2
                    wait_unit(u, i, 12)
                    pe.wait_ge(hid_ready, i * 4 + (e + 3))
                    w = slot(u, D)
                    for r in range(8):
                        n, t = r // 2, r % 2
                        pe.wait_ge(moe_added, i * 32 + (8 * e + r + 1))
                        for f in range(2):
                            mm = pe.matmul(bank[4 + r % 4][:, :], HID[:, e % 2, f, t * P:(t + 1) * P],
                                           w[:, f, n * CH:(n + 1) * CH], start=f == 0, stop=f == 1)
                        mm.then_inc(w_used if r == 7 else down_done, 1)

            turn_norm(4)
            pe.wait_ge(ple_loaded, 32)
            turn(PIN, 0, 256)
            pe.wait_ge(turn_kept, turns)
            for n in range(4):
                q = QCH + n
                if n >= 2:
                    pe.wait_ge(out_ready, n - 1)
                for t in range(T2):
                    for k in range(2):
                        mm = pe.matmul(bank[4 + 2 * (n % 2) + t][:, :], PINT[:, t, k * P:(k + 1) * P],
                                       WUP[:, k, n * CH:(n + 1) * CH], start=k == 0, stop=k == 1)
                mm.then_inc(up_done, 1)
                wait_set(q)
                for j in range(2):
                    unit_natural(UH + 2 * n + j, bank[2 * (q % 2):2 * (q % 2) + 2], xt, 8 * j, 8, j == 0, j == 1)

        @block.scalar
        def _(act):
            def root_mean_square(ready, value, done):
                act.wait_ge(ready, value)
                for t in range(T2):
                    act.activation(XS[:, t, :], H[:, t, :], ACT.Square, accum_out=ss[:, t:t + 1])
                act.drain()
                act.activation(rms, ss, ACT.Sqrt, scale=1.0 / D, bias=eps).then_inc(done, 1)

            def keep_norm(j):
                for k in range(0, KC, 2):
                    act.wait_ge(x_turned, KC * j + k + 1)
                    act.activation(XT[:, :, k * P:(k + 1) * P], bank[4 + k % 4][:, 0:256].rearrange("p (t s) -> p t s", t=2),
                                   ACT.Copy, scale=GT[:, 16 * j + k:16 * j + k + 1]).then_inc(xt_act, 1)

            turns = 0

            def keep_turned(buf, dst, n):
                nonlocal turns
                for c in range(0, n, 256):
                    act.wait_ge(turned, turns + 1)
                    act.activation(buf[:, :, dst + c:dst + c + 256],
                                   bank[4 + turns % 4][:, :].rearrange("p (t s) -> p t s", t=2), ACT.Copy).then_inc(turn_kept, 1)
                    turns += 1

            def exps(n):
                _, _, _, _, sm, _ = att(n)
                _, _, nk = group(n)
                act.wait_ge(scores_ready, n + 1)
                for hh in range(4):
                    act.activation(sm[:, hh, 0:nk], sm[:, hh, 0:nk], ACT.Exp, bias=nmx[:, hh:hh + 1],
                                   accum_out=rs[:, hh:hh + 1]).then_inc(exp_ready, 1)
                if n < 4:
                    act.activation(es, es, ACT.Exp).then_inc(exp_ready, 1)
                else:
                    act.activation(es, nmx, ACT.Copy).then_inc(exp_ready, 1)

            def keep_probs(n):
                _, _, _, _, _, pt = att(n)
                _, _, nk = group(n)
                act.wait_ge(probs_turned, n + 1)
                for kt in range(nk // P):
                    last = act.activation(pt[:, kt, :], bank[6 + kt][:, :], ACT.Copy)
                    if kt == nk // P - 1:
                        last.then_inc(probs_kept, 1)

            def keep_attended(n):
                buf, cq, _, _, _, _ = att(n)
                h0, t, _ = group(n)
                act.wait_ge(attended, n + 1)
                act.activation(buf[:, t, cq + h0 * P:cq + h0 * P + CH], bank[4][:, :], ACT.Copy).then_inc(attn_kept, 1)

            act.wait_ge(c_loaded, 16)
            root_mean_square(x_loaded, 16, rms_ready)
            act.wait_ge(gt_ready, 2)
            keep_norm(0)
            for u in range(UB + 28):
                if u < UB and u % 2:
                    c = u // 2
                    act.wait_ge(w_used, u + 1)
                    for t in range(T2):
                        act.activation(P1[:, t, c * CH:(c + 1) * CH], bank[2 * (c % 2) + t][:, :],
                                       ACT.Silu if c * CH >= GR else ACT.Copy).then_inc(set_free, 1)
                for step in AFTER1.get(u, ()):
                    if step[0] == "tr":
                        keep_turned(P1, step[2], step[3])
                    elif step[0] == "S":
                        exps(step[1])
                    elif step[0] == "T":
                        keep_probs(step[1])
                    elif step[0] == "V":
                        keep_attended(step[1])
                    elif step[0] == "R":
                        i = step[1]
                        if i < HEADS:
                            act.wait_ge(ret_inner, i + 1)
                            act.activation(KV[:, i % 2, :], bank[5][:, 0:256], ACT.Copy).then_inc(state_ready, 1)
                        if i:
                            act.wait_ge(ret_stats, i)
                            act.activation(P1[:, :, VR + 256 * (i - 1):VR + 256 * i],
                                           bank[6 + (i - 1) % 2][:, :].rearrange("p (t s) -> p t s", t=2),
                                           ACT.Copy).then_inc(ret_kept, 1)
                    elif step[0] == "rnorm":
                        act.wait_ge(var_ready, 1)
                        act.activation(ORMS, MV[:, :, 1], ACT.Sqrt, bias=eps).then_inc(ret_rms, 1)
                    elif step[0] == "gate":
                        _, n, which = step
                        act.wait_ge(w_used, u + 1)
                        if n:
                            act.wait_ge(merged, n)
                        q = QCB + 2 * n + which
                        for t in range(T2):
                            act.activation(XSf[:, (2 * which + t) * CH:(2 * which + t + 1) * CH],
                                           bank[2 * (q % 2) + t][:, :], ACT.Sigmoid).then_inc(set_free, 1)

            root_mean_square(set_free, CREDITS + 2 * QCD, rms_ready)
            keep_norm(1)
            with act.Fori(0, 2) as i:
                for c in range(2):
                    act.wait_ge(w_used, i * 4 + (UD + 2 * c + 2))
                    for half in range(2):
                        act.activation(QT[:, :, ds(i * (2 * CH) + (c * CH + half * 256), 256)].rearrange("p t (b n) -> p b t n", b=2),
                                       bank[2 * ((QCD + c) % 2) + half][:, :].rearrange("p (b t s) -> p b t s", b=2, t=2),
                                       ACT.Copy).then_inc(set_free, 1)
            act.wait_ge(keys_turned, 1)
            for b in range(4):
                act.activation(KT[:, 4 * b:4 * b + 4, :], bank[4 + b][:, :].rearrange("p (b n) -> p b n", b=4),
                               ACT.Copy).then_inc(keys_kept, 1)
            for r in range(8):
                act.wait_ge(peer_scored, r + 1)
                act.activation(S[:, r // 4, 4 * (r % 4):4 * (r % 4) + 4, :], bank[4 + r % 4][:, :].rearrange("p (b n) -> p b n", b=4),
                               ACT.Copy).then_inc(s_kept, 1)
            for t in range(T2):
                act.wait_ge(best_ready, t + 1)
                act.activation(gate_all[:, t, :], gate_all[:, t, :], ACT.Exp).then_inc(gate_exp, 1)
            gate_cur = small[:, 80:96]
            for t in range(T2):
                act.wait_ge(idx_ready, t + 1)
                with act.Fori(0, HEADS) as h:
                    act.wait_ge(added, h * TOPK + (4 + P * t))
                    act.activation(gate_cur, gate_all[:, t, ds(h * TOPK, TOPK)], ACT.Copy)
                    for j in range(TOPK):
                        act.wait_ge(dotted, h * TOPK + (P * t + j + 5))
                        act.activation(acts[:, j:j + 1], dots[:, j:j + 1], ACT.Gelu)
                        act.drain()
                        act.activation(wts[:, j:j + 1], acts[:, j:j + 1], ACT.Copy,
                                       scale=gate_cur[:, j:j + 1]).then_inc(weight_ready, 1)
            root_mean_square(peer_done, 1, fin_rms)

            root_mean_square(x2_ready, 2, rms_ready)
            keep_norm(2)
            for c, (kind, n) in enumerate(CHUNK_E):
                q = QCE + c
                for half in range(2):
                    if half:
                        act.wait_ge(w_used, UE + 2 * c + 2)
                        for t in range(T2):
                            ps = bank[2 * (q % 2) + t]
                            pair = ps[:, :].rearrange("p (b s) -> p b s", b=2)
                            if kind == "rx":
                                o = act.activation(RX[:, 4 * n + 2 * t:4 * n + 2 * t + 2, 4:RXP], pair, ACT.Copy)
                            elif kind == "rg":
                                o = act.activation(GELU[:, 4 * n + 2 * t:4 * n + 2 * t + 2, :], pair, ACT.Gelu_apprx_tanh)
                            else:
                                at = {"q": Q2, "k": K2, "v": V2}[kind] + n * CH
                                o = act.activation(P2[:, t, at:at + CH], ps[:, :], ACT.Copy)
                            o.then_inc(set_free, 1)
                    for step in AFTER2.get(2 * c + half, ()):
                        if step[0] == "tr":
                            keep_turned(P2, step[2], step[3])
                        elif step[0] == "S":
                            exps(step[1])
                        elif step[0] == "T":
                            keep_probs(step[1])
                        elif step[0] == "V":
                            keep_attended(step[1])
                        elif step[0] == "FL":
                            act.wait_ge(sp_in, 1)
                            act.activation(SPZ, SPA, ACT.Exp, scale=-1.0).then_inc(sp_exp, 1)
                        elif step[0] == "LG":
                            act.wait_ge(lru_mm, step[1] + 1)
                            for b in range(8):
                                act.activation((IGATE if step[1] else RGATE)[:, b, :],
                                               bank[4 + b // 2][:, (b % 2) * 256:(b % 2 + 1) * 256], ACT.Sigmoid,
                                               bias=(b_ing if step[1] else b_rec)[:, b:b + 1]).then_inc(gates_ready, 1)
                        elif step[0] == "lru":
                            act.wait_ge(sp_done, 1)
                            act.drain()
                            for b in range(8):
                                act.activation(DECAY_A[:, b, :], RGATE[:, b, :], ACT.Exp, scale=lru_neg[:, b:b + 1])
                            act.drain()
                            for b in range(8):
                                act.activation(RGATE[:, b, :], RGATE[:, b, :], ACT.Tanh,
                                               scale=lru_pos[:, b:b + 1]).then_inc(decay_ready, 1)
                            act.wait_ge(gap_ready, 1)
                            act.activation(TMP, TMP, ACT.Sqrt).then_inc(gap_root, 1)
                        elif step[0] == "FC":
                            act.wait_ge(cum_done, 1)
                            act.activation(CT[0:8, :], bank[5][0:8, 0:256], ACT.Copy).then_inc(cum_kept, 1)
                        elif step[0] == "qknorm":
                            act.wait_ge(hsq_ready, step[1] + 1)
                            act.activation(hrms, hrms, ACT.Sqrt, scale=1.0 / HD, bias=eps).then_inc(hrms_ready, 1)

            root_mean_square(set_free, CREDITS + 2 * QCH, rms_ready)
            keep_norm(3)
            act.wait_ge(route_in, 1)
            act.activation(GEXP, GEXP, ACT.Exp)
            act.activation(RSC[:, :, 0:1], RSC[:, :, 0:1], ACT.Exp).then_inc(route_exp, 1)
            with act.Fori(0, EXPERTS // 4) as i:
                for e in range(4):
                    act.wait_ge(w_used, i * 12 + (UG + 3 * e + 2))
                    act.wait_ge(hid_ready, i * 4 + (e + 1))
                    act.activation(XSf[:, (e % 2) * CH:(e % 2 + 1) * CH], bank[2 * (e % 2)][:, :], ACT.Silu).then_inc(silu_ready, 1)

            root_mean_square(moe_added, 4 + 8 * EXPERTS, rms_ready)
            keep_norm(4)
            keep_turned(PINT, 0, 256)
            for n in range(4):
                act.wait_ge(w_used, UH + 2 * n + 2)
                if n >= 2:
                    act.wait_ge(out_ready, n - 1)
                for t in range(T2):
                    act.activation(XSf[:, (2 * (n % 2) + t) * CH:(2 * (n % 2) + t + 1) * CH],
                                   bank[2 * ((QCH + n) % 2) + t][:, :], ACT.Sigmoid).then_inc(set_free, 1)

        @block.vector
        def _(dve):
            TT, TS, STT = dve.tensor_tensor, dve.tensor_scalar, dve.scalar_tensor_tensor

            def scale_norm(j):
                dve.wait_ge(rms_ready, j + 1)
                dve.reciprocal(rstd, rms)
                dve.drain()
                for t in range(T2):
                    TS(XS[:, t, :], H[:, t, :], rstd[:, t:t + 1], None, ALU.mult).then_inc(xs_ready, 1)
                for k in range(1, KC, 2):
                    dve.wait_ge(x_turned, KC * j + k + 1)
                    TS(XT[:, :, k * P:(k + 1) * P], bank[4 + k % 4][:, 0:256].rearrange("p (t s) -> p t s", t=2),
                       GT[:, 16 * j + k:16 * j + k + 1], None, ALU.mult).then_inc(xt_dve, 1)

            def rope(at, heads):
                x = P1[:, :, at:at + heads * HD].rearrange("p t (h d) -> p t h d", d=HD)
                x1, x2 = x[:, :, :, 0:64], x[:, :, :, 64:128]
                n = 2 * heads * 64
                a, b = (XSf[:, j * 1024:j * 1024 + n].rearrange("p (t h d) -> p t h d", t=2, d=64) for j in range(2))
                c, s = (v.unsqueeze(2).to_broadcast([P, 2, heads, 64]) for v in (cos, sin))
                TT(a, x1, s, ALU.mult)
                TT(b, x2, s, ALU.mult)
                dve.drain()
                TT(x1, x1, c, ALU.mult)
                TT(x2, x2, c, ALU.mult)
                dve.drain()
                TT(x1, x1, b, ALU.subtract)
                return TT(x2, x2, a, ALU.add)

            def prepare(n):
                _, _, _, _, sm, _ = att(n)
                h0, t, nk = group(n)
                dve.wait_ge(scored, n + 1)
                mask = const("wmask" if n < 4 else "cmask")[:, 256 - nk:256]
                for b in range(2):
                    o = sm[:, 2 * b:2 * b + 2, 0:nk]
                    s = bank[4 + b][:, :].rearrange("p (h k) -> p h k", h=2)[:, :, 0:nk]
                    if n < 4:
                        STT(o, s, HD ** -0.5, mask.unsqueeze(1).to_broadcast([P, 2, nk]), ALU.mult, ALU.add)
                    else:
                        for hh in range(2):
                            h = h0 + 2 * b + hh
                            STT(o[:, hh, :], s[:, hh, :], CUM[:, t, h:h + 1], mask, ALU.add, ALU.add)
                dve.drain()
                dve.tensor_reduce(mx, sm[:, :, 0:nk], AX, ALU.max)
                dve.drain()
                if n < 4:
                    TT(mx, mx, sinks[:, h0:h0 + 4], ALU.max)
                    dve.drain()
                    TT(es, sinks[:, h0:h0 + 4], mx, ALU.subtract)
                TS(nmx, mx, -1.0, None, ALU.mult).then_inc(scores_ready, 1)
                dve.wait_ge(exp_ready, 5 * (n + 1))
                if n < 4:
                    TT(rden, rs, es, ALU.add)
                    dve.drain()
                    dve.reciprocal(rden, rden)
                else:
                    dve.reciprocal(rden, rs)
                dve.drain()
                TT(sm[:, :, 0:nk], sm[:, :, 0:nk], rden.unsqueeze(2).to_broadcast([P, 4, nk]), ALU.mult).then_inc(probs_ready, 1)

            dve.sem_inc(set_free, CREDITS)
            dve.wait_ge(c_loaded, 16)
            dve.wait_ge(g_loaded, 17 * 16)
            dve.wait_ge(gt_turned, 1)
            dve.tensor_copy(GT[:, 0:80], bank[4][:, 0:80]).then_inc(gt_ready, 1)
            dve.tensor_copy(GT[:, 80:144], bank[5][:, 0:64]).then_inc(gt_ready, 1)
            dve.wait_ge(gt_ready, 2)
            scale_norm(0)
            for u in range(UB + 28):
                for step in AFTER1.get(u, ()):
                    if step[0] == "rope":
                        which = step[1]
                        at, heads, chunks = ((QA, 8, 2), (KA, 2, 3), (QR, 8, 5), (KR, 8, 7))[which]
                        dve.wait_ge(set_free, CREDITS + 2 * chunks)
                        last = rope(at, heads)
                        if which >= 2:
                            dve.drain()
                            dec = const("qdecay" if which == 2 else "kdecay")
                        if which == 2:
                            x = P1[:, :, QR:QR + 1024].rearrange("p t (h d) -> p t h d", d=HD)
                            last = TT(x, x, dec.unsqueeze(1).unsqueeze(3).to_broadcast([P, 2, 8, HD]), ALU.mult)
                        if which == 3:
                            x = P1[:, 0, KR:KR + 1024].rearrange("p (h d) -> p h d", d=HD)
                            last = TT(KDEC, x, dec.unsqueeze(2).to_broadcast([P, 8, HD]), ALU.mult)
                        last.then_inc(roped, 1)
                        dve.wait_ge(roped, which + 1)
                    elif step[0] == "S":
                        prepare(step[1])
                    elif step[0] == "R":
                        i = step[1]
                        if i < HEADS:
                            dve.wait_ge(ret_inner, i + 1)
                            dec = const("decay")[:, i * P:(i + 1) * P]
                            TT(IN[:, i % 2, :, :], bank[4][:, 0:256].rearrange("p (t c) -> p t c", t=2),
                               dec.unsqueeze(1).to_broadcast([P, 2, P]), ALU.mult).then_inc(inner_ready, 1)
                        if i:
                            dve.wait_ge(ret_out, i)
                            for t in range(T2):
                                last = dve.bn_stats(STATS[:, 2 * (i - 1) + t, :], bank[6 + (i - 1) % 2][:, t * 256:(t + 1) * 256])
                            last.then_inc(ret_stats, 1)
                    elif step[0] == "rnorm":
                        dve.drain()
                        for g in range(16):
                            last = dve.bn_aggr(MV[:, g, :], STATS[:, g, :])
                        last.then_inc(var_ready, 1)
                        dve.wait_ge(ret_rms, 1)
                        dve.reciprocal(ORSTD, ORMS)
                        dve.wait_ge(ret_kept, HEADS)
                        dve.drain()
                        for g in range(16):
                            o = P1[:, g % 2, VR + 256 * (g // 2):VR + 256 * (g // 2 + 1)]
                            TS(o, o, MV[:, g, 0:1], ORSTD[:, g:g + 1], ALU.subtract, ALU.mult)
                        dve.drain()
                        dve.wait_ge(set_free, CREDITS + 2 * QCB)
                        TT(P1[:, :, GR:GR + D], P1[:, :, VR:VR + D], P1[:, :, GR:GR + D], ALU.mult).then_inc(ret_ready, 1)
                    elif step[0] == "merge":
                        n = step[1]
                        dve.wait_ge(w_used, u + 1)
                        dve.wait_ge(set_free, CREDITS + 2 * (QCB + 2 * n + 2))
                        if n == 0:
                            dve.wait_ge(ret_ready, 1)
                        for t in range(T2):
                            TT(XSf[:, t * CH:(t + 1) * CH], XSf[:, t * CH:(t + 1) * CH], bank[4 + t][:, :], ALU.mult)
                            TT(XSf[:, (2 + t) * CH:(3 + t) * CH], XSf[:, (2 + t) * CH:(3 + t) * CH], bank[6 + t][:, :], ALU.mult)
                        dve.drain()
                        m = P1[:, :, VR + n * CH:VR + (n + 1) * CH]
                        TT(m, XSf[:, 0:1024].rearrange("p (t n) -> p t n", t=2),
                           XSf[:, 1024:2048].rearrange("p (t n) -> p t n", t=2), ALU.add).then_inc(merged, 1)

            def add_square(u0, q0):
                with dve.Fori(0, 2) as i:
                    for c in range(2):
                        dve.wait_ge(w_used, i * 4 + (u0 + 2 * c + 2))
                        for t in range(T2):
                            h = H[:, t, ds(i * (2 * CH) + c * CH, CH)]
                            TT(h, bank[2 * ((q0 + c) % 2) + t][:, :], h, ALU.add).then_inc(set_free, 1)

            add_square(UC, QCC)

            scale_norm(1)
            dve.wait_ge(grow_loaded, 16)
            for t in range(T2):
                TT(HN[:, t, :], XS[:, t, :], GROW, ALU.mult).then_inc(hn_ready, 1)
            for t in range(T2):
                dve.wait_ge(s_kept, 4 * (t + 1))
                blocks = [(h, q) for h in range(HEADS) for q in range(2)]
                for half in range(2):
                    lo = 8 * half
                    for h, q in blocks:
                        dve.max(TV[:, t, h, q, lo:lo + 8], S[:, t, 2 * h + q, :])
                    dve.drain()
                    for h, q in blocks:
                        dve.max_index(TIU[:, t, h, q, lo:lo + 8], TV[:, t, h, q, lo:lo + 8], S[:, t, 2 * h + q, :])
                    if half == 0:
                        dve.drain()
                        for h, q in blocks:
                            dve.match_replace(S[:, t, 2 * h + q, :], TV[:, t, h, q, 0:8], S[:, t, 2 * h + q, :], LOWEST)
                    dve.drain()
                dve.wait_ge(s_kept, 8)
                dve.tensor_copy(TIF[:, t, :, :, :], TIU[:, t, :, :, :])
                TT(CAND[:, :, :].rearrange("p h (i j) -> p h i j", i=16),
                   TV[:, t, :, 0, :].unsqueeze(3).to_broadcast([P, 8, 16, 16]),
                   TV[:, t, :, 1, :].unsqueeze(2).to_broadcast([P, 8, 16, 16]), ALU.add)
                dve.drain()
                for half in range(2):
                    lo = 8 * half
                    for h in range(HEADS):
                        dve.max(BV[:, t, h, lo:lo + 8], CAND[:, h, :])
                    dve.drain()
                    for h in range(HEADS):
                        dve.max_index(PU[:, 0, h, lo:lo + 8], BV[:, t, h, lo:lo + 8], CAND[:, h, :])
                    if half == 0:
                        dve.drain()
                        for h in range(HEADS):
                            dve.match_replace(CAND[:, h, :], BV[:, t, h, 0:8], CAND[:, h, :], LOWEST)
                    dve.drain()
                g = gate_all[:, t, :].rearrange("p (h k) -> p h k", h=8)
                TT(g, BV[:, t, :, :], BV[:, t, :, 0:1].to_broadcast([P, 8, 16]), ALU.subtract).then_inc(best_ready, 1)
                TS(PU[:, 1, :, :], PU[:, 0, :, :], 4, None, ALU.logical_shift_right)
                TS(PU[:, 2, :, :], PU[:, 0, :, :], 15, None, ALU.bitwise_and)
                dve.drain()
                dve.tensor_copy(PF[:, 0:2, :, :], PU[:, 1:3, :, :])
                dve.drain()
                iota = const("iota16").unsqueeze(1).unsqueeze(1).to_broadcast([P, 8, 16, 16])
                for q in range(2):
                    TT(HOT, PF[:, q, :, :].unsqueeze(3).to_broadcast([P, 8, 16, 16]), iota, ALU.is_equal)
                    dve.drain()
                    TT(HOT, HOT, TIF[:, t, :, q, :].unsqueeze(2).to_broadcast([P, 8, 16, 16]), ALU.mult)
                    dve.drain()
                    dve.tensor_reduce(PF[:, 2 + q, :, :], HOT, AX, ALU.add)
                    dve.drain()
                STT(idx_all[:, t, :].rearrange("p (h k) -> p h k", h=8), PF[:, 2, :, :], 128.0, PF[:, 3, :, :], ALU.mult, ALU.add)
                dve.wait_ge(gate_exp, t + 1)
                dve.tensor_reduce(small[:, 96 + 8 * t:104 + 8 * t], g, AX, ALU.add)
                dve.drain()
                dve.reciprocal(small[:, 96 + 8 * t:104 + 8 * t], small[:, 96 + 8 * t:104 + 8 * t])
                dve.drain()
                TT(g, g, small[:, 96 + 8 * t:104 + 8 * t].unsqueeze(2).to_broadcast([P, 8, 16]), ALU.mult).then_inc(idx_ready, 1)
            dve.sem_inc(dotted, 4)
            dve.sem_inc(added, 4)
            dve.wait_ge(xt_act, 16)
            for t in range(T2):
                def add_up(h, j):
                    dve.wait_ge(weight_ready, h * TOPK + (P * t + j + 1))
                    dve.wait_ge(up_in[j % 4], h * 64 + 16 * ((P * t + j) // 4 + 1))
                    dve.wait_ge(added, h * TOPK + (P * t + j + 4))
                    STT(H[:, t, :], W[:, 2 + j % 4 // 2, (j % 2) * D:(j % 2 + 1) * D], wts[:, j:j + 1],
                        H[:, t, :], ALU.mult, ALU.add).then_inc(added, 1)

                with dve.Fori(0, HEADS) as h:
                    for j in range(TOPK):
                        dve.wait_ge(down_in[j % 4], h * 64 + 16 * ((P * t + j) // 4 + 1))
                        dve.wait_ge(dotted, h * TOPK + (P * t + j + 3))
                        dve.tensor_tensor_reduce(out=XT[:, j % 2, :], in0=W[:, j % 4 // 2, (j % 2) * D:(j % 2 + 1) * D],
                                                 in1=HN[:, t, :], scale=1.0, scalar=0.0, op0=ALU.mult, op1=ALU.add,
                                                 accum_out=dots[:, j:j + 1]).then_inc(dotted, 1)
                        if j >= 2:
                            add_up(h, j - 2)
                    add_up(h, TOPK - 2)
                    add_up(h, TOPK - 1)
            dve.wait_ge(added, 4 + T2 * P)
            dve.sem_inc(peer_done, 1)

            dve.wait_ge(fin_rms, 1)
            dve.reciprocal(rstd, rms)
            dve.wait_ge(grow_loaded, 32)
            dve.drain()
            for t in range(T2):
                STT(H[:, t, :], H[:, t, :], rstd[:, t:t + 1], GROW, ALU.mult, ALU.mult).then_inc(x2_ready, 1)
            dve.wait_ge(x2_ready, 2)
            scale_norm(2)
            dve.memset(RX[:, :, 0:4], 0.0)
            dve.memset(CT, 0.0)
            dve.drain()
            for u in range(20):
                for step in AFTER2.get(u, ()):
                    if step[0] == "FL":
                        dve.wait_ge(fl_done, 1)
                        TT(SPV[:, 0:16].rearrange("p (t h) -> p t h", t=2), bank[4][:, 0:16].rearrange("p (t h) -> p t h", t=2),
                           b_forget.unsqueeze(1).to_broadcast([P, 2, 8]), ALU.add)
                        dve.tensor_copy(SPV[:, 16:24], lam)
                        dve.drain()
                        STT(SPA, SPV, -1.0, SPV, ALU.mult, ALU.max).then_inc(sp_in, 1)
                        dve.wait_ge(sp_exp, 1)
                        TS(SPS, SPZ, 2.0, None, ALU.add)
                        dve.drain()
                        dve.reciprocal(SPS, SPS)
                        dve.drain()
                        TT(SPS, SPS, SPZ, ALU.mult)
                        dve.drain()
                        TT(SPQ, SPS, SPS, ALU.mult)
                        dve.drain()
                        TS(SPA, SPQ, 1.0 / 17.0, None, ALU.mult)
                        for m in (15, 13, 11, 9, 7, 5, 3):
                            dve.drain()
                            STT(SPA, SPA, 1.0 / m, SPQ, ALU.add, ALU.mult)
                        dve.drain()
                        STT(SPA, SPA, 1.0, SPS, ALU.add, ALU.mult)
                        TS(SPV, SPV, -1.0, 0.0, ALU.mult, ALU.max)
                        dve.drain()
                        STT(SPA, SPA, 2.0, SPV, ALU.mult, ALU.add)
                        dve.drain()
                        TS(LF, SPA[:, 0:16].rearrange("p (t h) -> p t h", t=2), -1.0, None, ALU.mult)
                        TS(lru_neg, SPA[:, 16:24], -8.0, None, ALU.mult)
                        TS(lru_pos, SPA[:, 16:24], 8.0, None, ALU.mult)
                        dve.drain()
                        dve.sem_inc(sp_done, 1)
                    elif step[0] == "conv":
                        dve.wait_ge(set_free, CREDITS + 2 * (QCE + 2))
                        for k in (3, 2, 1, 0):
                            for b in range(8):
                                x = RX[:, b, 1 + k:257 + k]
                                if k == 3:
                                    TS(XC[:, b, :], x, conv_w[:, k, b:b + 1], conv_b[:, b:b + 1], ALU.mult, ALU.add)
                                else:
                                    STT(XC[:, b, :], x, conv_w[:, k, b:b + 1], XC[:, b, :], ALU.mult, ALU.add)
                            dve.drain()
                        dve.sem_inc(conv_ready, 1)
                    elif step[0] == "lru":
                        dve.wait_ge(decay_ready, 8)
                        TT(TMP, DECAY_A, DECAY_A, ALU.mult)
                        dve.wait_ge(gates_ready, 16)
                        TT(IGATE, IGATE, XC, ALU.mult)
                        dve.drain()
                        STT(TMP, TMP, 1.0, RGATE, ALU.add, ALU.mult).then_inc(gap_ready, 1)
                        dve.wait_ge(gap_root, 1)
                        TT(IGATE, IGATE, TMP, ALU.mult)
                        dve.drain()
                        for b in range(8):
                            dve.tensor_tensor_scan(TMP[:, b, :], DECAY_A[:, b, :], IGATE[:, b, :], 0.0, ALU.mult, ALU.add)
                        dve.drain()
                    elif step[0] == "gelu":
                        dve.wait_ge(set_free, CREDITS + 2 * QCF)
                        TT(PX.rearrange("p t (b s) -> p b t s", s=P), TMP.rearrange("p b (t s) -> p b t s", t=2),
                           GELU.rearrange("p b (t s) -> p b t s", t=2), ALU.mult).then_inc(rnn_ready, 1)
                    elif step[0] == "FC":
                        dve.wait_ge(cum_done, 1)
                        dve.tensor_copy(CUM, bank[4][:, 0:16].rearrange("p (t h) -> p t h", t=2)).then_inc(cum_kept, 1)
                    elif step[0] == "qknorm":
                        which = step[1]
                        dve.wait_ge(set_free, CREDITS + 2 * (QCE + 4 + 2 * which))
                        x = P2[:, :, which * 1024:(which + 1) * 1024]
                        sq = XSf[:, 0:2048].rearrange("p (t n) -> p t n", t=2)
                        TT(sq, x, x, ALU.mult)
                        dve.drain()
                        dve.tensor_reduce(hrms, sq.rearrange("p t (h d) -> p t h d", d=HD), AX, ALU.add).then_inc(hsq_ready, 1)
                        dve.wait_ge(hrms_ready, which + 1)
                        dve.reciprocal(hrstd, hrms)
                        dve.drain()
                        if which == 0:
                            TS(hrstd, hrstd, HD ** -0.5, None, ALU.mult)
                            dve.drain()
                        xh = x.rearrange("p t (h d) -> p t h d", d=HD)
                        TT(xh, xh, hrstd.unsqueeze(3).to_broadcast([P, 2, 8, HD]), ALU.mult)
                        dve.drain()
                        xg = x.rearrange("p t (h d) -> p (t) h d", d=HD)
                        TT(xg, xg, qk_gain[which].unsqueeze(1).unsqueeze(1).to_broadcast([P, 2, 8, HD]), ALU.mult).then_inc(qk_ready, 1)
                    elif step[0] == "S":
                        prepare(step[1])
            add_square(UF, QCF)

            dve.sem_inc(hid_ready, 2)
            dve.sem_inc(moe_added, 4)
            dve.memset(RL[:, :, 4:8], LOWEST)
            scale_norm(3)
            dve.wait_ge(routed, 1)
            logits = bank[4][:, 0:128].rearrange("p (t e) -> p t e", t=2)
            dve.tensor_copy(RL[:, :, 0:4], logits[:, :, 0:4])
            dve.tensor_copy(RL[:, :, 8:40], logits[:, :, 4:36])
            dve.drain()
            for g in range(2):
                seen = RL[:, :, 0:8] if g == 0 else ML
                for t in range(T2):
                    dve.max(TOPV[:, t, g, :], seen[:, t, :])
                dve.drain()
                for t in range(T2):
                    dve.max_index(TOPU[:, t, g, :], TOPV[:, t, g, :], seen[:, t, :])
                dve.drain()
                dve.tensor_copy(TOPF[:, :, g, :], TOPU[:, :, g, :])
                dve.drain()
                if g == 0:
                    pick, drop = RSC[:, :, 4:8], HOT32[:, :, 0:4]
                    for t in range(T2):
                        TS(pick[:, t, :], const("iota16")[:, 0:4], TOPF[:, t, 0, 0:1], None, ALU.is_equal)
                    dve.drain()
                    TS(drop, pick, -1.0, -LOWEST, ALU.add, ALU.mult)
                    m = ML.rearrange("p t (g e) -> p t g e", g=4)
                    TT(m, RL[:, :, 8:40].rearrange("p t (g e) -> p t g e", g=4), pick.unsqueeze(3).to_broadcast([P, 2, 4, 8]), ALU.mult)
                    dve.drain()
                    TT(m, m, drop.unsqueeze(3).to_broadcast([P, 2, 4, 8]), ALU.add)
                    dve.drain()
            for t in range(T2):
                TS(GEXP[:, t, :], RL[:, t, 0:4], TOPV[:, t, 0, 0:1], None, ALU.subtract)
            TT(RSC[:, :, 0:1], TOPV[:, :, 1, 1:2], TOPV[:, :, 1, 0:1], ALU.subtract)
            dve.drain()
            dve.sem_inc(route_in, 1)
            dve.wait_ge(route_exp, 1)
            dve.tensor_reduce(RSC[:, :, 1], GEXP, AX, ALU.add)
            TS(RSC[:, :, 2:3], RSC[:, :, 0:1], 1.0, None, ALU.add)
            dve.drain()
            dve.reciprocal(RSC[:, :, 1:3], RSC[:, :, 1:3])
            dve.drain()
            TT(RSC[:, :, 2:3], RSC[:, :, 2:3], RSC[:, :, 1:2], ALU.mult)
            dve.drain()
            TT(RSC[:, :, 3:4], RSC[:, :, 2:3], RSC[:, :, 0:1], ALU.mult)
            dve.drain()
            for t in range(T2):
                TS(COMB[:, t, :], const("iota32"), TOPF[:, t, 1, 0:1], RSC[:, t, 2:3], ALU.is_equal, ALU.mult)
                TS(HOT32[:, t, :], const("iota32"), TOPF[:, t, 1, 1:2], RSC[:, t, 3:4], ALU.is_equal, ALU.mult)
            dve.drain()
            TT(COMB, COMB, HOT32, ALU.add).then_inc(comb_ready, 1)
            dve.wait_ge(comb_ready, 1)
            weight = small[:, 512:520].rearrange("p (t e) -> p t e", t=2)
            with dve.Fori(0, EXPERTS // 4) as i:
                dve.drain()
                dve.tensor_copy(weight, COMB[:, :, ds(i * 4, 4)])
                dve.drain()
                for e in range(4):
                    dve.wait_ge(silu_ready, i * 4 + (e + 1))
                    TT(HID[:, e % 2, :, :], XSf[:, (e % 2) * CH:(e % 2 + 1) * CH].rearrange("p (f s) -> p f s", f=2),
                       bank[2 * (e % 2) + 1][:, :].rearrange("p (f s) -> p f s", f=2), ALU.mult).then_inc(hid_ready, 1)
                    for r in range(8):
                        n, t = r // 2, r % 2
                        if r < 7:
                            dve.wait_ge(down_done, i * 28 + (7 * e + r + 1))
                        else:
                            dve.wait_ge(w_used, i * 12 + (UG + 3 * e + 3))
                        h = H[:, t, n * CH:(n + 1) * CH]
                        STT(h, bank[4 + r % 4][:, :], weight[:, t, e:e + 1], h, ALU.mult, ALU.add).then_inc(moe_added, 1)

            dve.wait_ge(moe_added, 4 + 8 * EXPERTS)
            scale_norm(4)
            for n in range(4):
                dve.wait_ge(set_free, CREDITS + 2 * (QCH + n + 1))
                dve.wait_ge(up_done, n + 1)
                x = XSf[:, 2 * (n % 2) * CH:2 * (n % 2 + 1) * CH].rearrange("p (t n) -> p t n", t=2)
                for t in range(T2):
                    TT(x[:, t, :], x[:, t, :], bank[4 + 2 * (n % 2) + t][:, :], ALU.mult)
                dve.drain()
                h = H[:, :, n * CH:(n + 1) * CH]
                TT(h, h, x, ALU.add).then_inc(out_ready, 1)


def constants():
    import numpy as np

    c = np.zeros((P, CONST_W), np.float32)

    def put(name, value):
        a, b = CONST_AT[name]
        c[:, a:b] = value

    row = np.arange(P)
    put("ident", np.eye(P))
    freq = (1.0 / (np.float32(10000.0) ** (np.arange(0, HD, 2, dtype=np.float32) / np.float32(HD)))).astype(np.float32)
    angle = (np.arange(2 * P, dtype=np.float32)[:, None] * freq[None, :]).astype(np.float32)
    for name, f in (("cos", np.cos), ("sin", np.sin)):
        put(name, f(angle).reshape(2, P, 64).transpose(1, 0, 2).reshape(P, 128))
    causal = np.where(row[None, :] <= row[:, None], 0.0, NEG)
    put("wmask", np.concatenate([np.where(row[None, :] > row[:, None], 0.0, NEG), causal], 1))
    put("cmask", np.concatenate([np.zeros((P, P)), causal], 1))
    gamma = 1.0 - 2.0 ** (-5.0 - np.arange(HEADS))
    lower = row[None, :] >= row[:, None]
    put("decay", np.concatenate([np.where(lower, g ** -(row[:, None] + 1.0) * HD ** -0.5, 0.0) for g in gamma], 1))
    put("qdecay", gamma[None, :] ** (row[:, None] + 1.0))
    put("kdecay", gamma[None, :] ** (P - 1.0 - row[:, None]) * HD ** -0.5)
    put("tri", np.concatenate([row[:, None] <= row[None, :], np.ones((P, P))], 1))
    sel = np.zeros((P, HEADS, P))
    for h in range(HEADS):
        sel[h, h, :] = -1.0
    put("sel", sel.reshape(P, -1))
    put("iota16", np.arange(16)[None, :])
    put("iota32", np.arange(32)[None, :])
    put("eps", EPS)
    return c


INPUTS = ["x", "attn_norm", "w_in", "attn_sinks", "w_attn_branch", "w_ret_branch", "w_out", "ffn_norm",
          "w_peer_query", "peer_sub_keys", "peer_expert_down", "peer_expert_up", "final_norm", "p_2",
          "mix_norm_2", "w_in_2", "b_forget_2", "q_norm_2", "k_norm_2", "conv_w_2", "conv_b_2",
          "w_rec_gate_2", "b_rec_gate_2", "w_in_gate_2", "b_in_gate_2", "lru_lambda_2", "w_out_2",
          "ffn_norm_2", "w_router_group_2", "w_router_expert_2", "w_expert_gate_2", "w_expert_up_2",
          "w_expert_down_2", "ple_norm_2", "w_ple_gate_2", "w_ple_up_2"]


def kernel(**inputs):
    import numpy as np
    import concourse.bacc as bacc
    from concourse.bass_utils import run_bass_kernel_spmd

    nc = bacc.Bacc("TRN2", target_bir_lowering=False, num_devices=1)
    arrays, aps = {}, {}
    for name in INPUTS:
        a = np.ascontiguousarray(inputs[name])
        arrays["in_" + name] = a
        aps[name] = nc.dram_tensor("in_" + name, a.shape, mybir.dt.from_np(a.dtype), kind="ExternalInput").ap()
    arrays["consts"] = constants()
    consts = nc.dram_tensor("consts", (P, CONST_W), mybir.dt.float32, kind="ExternalInput").ap()
    out = nc.dram_tensor("out", (1, 2 * P, D), mybir.dt.float32, kind="ExternalOutput").ap()
    two_blocks(nc, aps, consts, out)
    r = run_bass_kernel_spmd(nc, [arrays], core_ids=[0])
    return r.results[0]["out"]
```

```python
import concourse.bass as bass
from concourse import mybir
from contextlib import ExitStack

P = 128
D = 2048
T2 = 2
KC = D // P
CH = 512
SLOTS = 4
UNIT = 4096
HEADS = 8
HD = 128
EXPERTS = 32
DE = 256
CAP = 64
PAIRS = EXPERTS // 2
PAIR_UNITS = 6
ROUND_UNITS = PAIRS * PAIR_UNITS
MAX_ROUNDS = 2 * P // CAP
TOPK = 16
EPS = 1e-6
NEG = -1e30
LOWEST = -3e38

QA, KA, VA, QR, KR, VR, GR, P1W = 0, 1024, 1280, 1536, 2560, 3584, 5632, 7680
GATE_A, GATE_R = P1W, P1W + D
Q2, K2, V2, RN2, P2W = 0, 1024, 2048, 3072, 4096
W2_F, W2_RX, W2_RG = 3072, 3080, 4104

UA, UB, UC, UD, UE, UF, UG = 0, 30, 58, 66, 74, 94, 102
QCA, QCB, QCC, QCD, QCE, QCF, QCH = 0, 15, 23, 27, 31, 41, 45
CREDITS = 4

CONST_AT = {}
CONST_W = 0
for _name, _width in (("ident", 128), ("cos", 128), ("sin", 128), ("wmask", 256), ("cmask", 256),
                      ("decay", 1024), ("qdecay", 8), ("kdecay", 8), ("tri", 256), ("sel", 1024),
                      ("iota64", 64), ("eps", 1)):
    CONST_AT[_name] = (CONST_W, CONST_W + _width)
    CONST_W += _width
CHUNK_E = [("rx", 0), ("rx", 1), ("q", 0), ("q", 1), ("k", 0), ("k", 1), ("v", 0), ("v", 1),
           ("rg", 0), ("rg", 1)]


def steps_of_first_block():
    after = {6: [("tr", QA, QA, 512)], 7: [("tr", QA + 512, QA + 512, 512)], 8: [("tr", KA, KA, 256)],
             9: [("S", 0)], 10: [("T", 0), ("V", 0), ("S", 1)], 11: [("T", 1), ("V", 1), ("S", 2)],
             12: [("T", 2), ("V", 2), ("S", 3)], 13: [("T", 3), ("V", 3)],
             15: [("tr", QR, QR, 512)], 16: [("tr", QR + 512, QR + 512, 512)],
             17: [("tr", KR, KR, 512)], 18: [("tr", KR + 512, KR + 512, 512)],
             3: [("rope", 0)], 5: [("rope", 1)], 14: [("rope", 2), ("rope", 3)],
             30: [("R", 8), ("rnorm", 0)],
             33: [("tr", GR + 512 * j, QR + 512 * j, 512) for j in range(4)]}
    for i in range(8):
        after[22 + i] = [("R", i)]
    for n in range(4):
        after.setdefault(UB + 7 * n + 1, []).append(("gate", n, 0))
        after.setdefault(UB + 7 * n + 3, []).append(("gate", n, 1))
        after[UB + 7 * n + 6] = [("merge", n)]
        if n:
            after[UB + 7 * n + 2] = [("tr", VR + 512 * (n - 1), GR + 512 * (n - 1), 512)]
    after[UB + 27].append(("tr", VR + 1536, GR + 1536, 512))
    return after


def steps_of_second_block():
    return {1: [("FL", 0)], 3: [("conv", 0)], 4: [("LG", 0)], 5: [("LG", 1), ("lru", 0)],
            6: [("FC", 0)], 7: [("qknorm", 0)], 9: [("tr", Q2, Q2, 512)],
            10: [("tr", Q2 + 512, Q2 + 512, 512)],
            11: [("qknorm", 1)], 13: [("tr", K2, K2, 512)], 14: [("tr", K2 + 512, K2 + 512, 512)],
            15: [("S", 4)], 16: [("T", 4), ("V", 4), ("S", 5)], 17: [("T", 5), ("V", 5), ("S", 6)],
            18: [("T", 6), ("V", 6), ("S", 7)], 19: [("T", 7), ("V", 7), ("gelu", 0)]}


def two_blocks(nc, A, consts, out):
    f32, u32 = mybir.dt.float32, mybir.dt.uint32
    ALU, ACT, AX = mybir.AluOpType, mybir.ActivationFunctionType, mybir.AxisListType.X
    AFTER1, AFTER2 = steps_of_first_block(), steps_of_second_block()
    ds = bass.ds

    ctx = ExitStack()
    with ctx:
        def sb(name, shape, dt=f32):
            return ctx.enter_context(nc.sbuf_tensor(name, shape, dt))

        def sem(name):
            return ctx.enter_context(nc.semaphore(name))

        H = sb("H", [P, T2, D])
        XT = sb("XT", [P, T2, D])
        XS = sb("XS", [P, T2, D])
        W = sb("W", [P, SLOTS, UNIT])
        big = sb("big", [P, 19456])
        C = sb("C", [P, CONST_W])
        gains_raw = big[:, 0:256].rearrange("p (a n) -> p a n", a=2)
        GT = sb("GT", [P, 144])
        WR = sb("WR", [P, KC, 36])
        WF = sb("WF", [P, KC, 8])
        rowc = sb("rowc", [P, 272])
        small = sb("small", [P, 640])
        idx_all = big[:, 4608:4864].bitcast(u32).rearrange("p (t n) -> p t n", t=2)
        gate_all = big[:, 4864:5120].rearrange("p (t n) -> p t n", t=2)
        idx_cur = sb("idx_cur", [P, 2, TOPK], u32)

        def const(name):
            return C[:, CONST_AT[name][0]:CONST_AT[name][1]]

        ident = const("ident")
        eps, iota = const("eps"), const("iota64")
        cos = const("cos").rearrange("p (t d) -> p t d", t=2)
        sin = const("sin").rearrange("p (t d) -> p t d", t=2)
        XSf = XS[:, :, :].rearrange("p t n -> p (t n)")
        sinks, b_forget = rowc[:, 0:8], rowc[:, 8:16]
        qk_gain = [rowc[:, 16:144], rowc[:, 144:272]]
        conv_w = GT[:, 80:112].rearrange("p (k n) -> p k n", k=4)
        conv_b, b_rec, b_ing, lam = (GT[:, 112 + 8 * j:120 + 8 * j] for j in range(4))

        P1 = big[:, 0:2 * P1W].rearrange("p (t n) -> p t n", t=2)
        KDEC = big[:, 15360:16384].rearrange("p (h d) -> p h d", h=8)
        IN = big[:, 18432:18944].rearrange("p (b t c) -> p b t c", b=2, t=2)
        KV = big[:, 18944:19456].rearrange("p (b e) -> p b e", b=2)
        QT = big[:, 0:4096].rearrange("p (t n) -> p t n", t=2)
        KT = big[:, 4096:6144].rearrange("p (b n) -> p b n", b=16)
        KEYS = big[:, 6144:8192].rearrange("p (b d) -> p b d", b=16)
        S = big[:, 8192:12288].rearrange("p (t b n) -> p t b n", t=2, b=16)
        HN = big[:, 12288:16384].rearrange("p (t n) -> p t n", t=2)
        GROW = big[:, 16384:18432]
        CAND = big[:, 0:2048].rearrange("p (h c) -> p h c", h=8)
        HOT = big[:, 2048:4096].rearrange("p (h b i) -> p h b i", h=8, b=16)
        PU = big[:, 4096:4608].bitcast(u32).rearrange("p (a h b) -> p a h b", a=4, h=8)
        TV = big[:, 6144:6656].rearrange("p (t h q k) -> p t h q k", t=2, h=8, q=2)
        TIU = big[:, 6656:7168].bitcast(u32).rearrange("p (t h q k) -> p t h q k", t=2, h=8, q=2)
        TIF = big[:, 7168:7680].rearrange("p (t h q k) -> p t h q k", t=2, h=8, q=2)
        BV = big[:, 7680:7936].rearrange("p (t h k) -> p t h k", t=2, h=8)
        PF = big[:, 18432:18944].rearrange("p (a h b) -> p a h b", a=4, h=8)
        P2 = big[:, 0:2 * P2W].rearrange("p (t n) -> p t n", t=2)
        RXP = 260
        RX = big[:, 8192:8192 + 8 * RXP].rearrange("p (b s) -> p b s", b=8)
        DECAY_A = RX[:, :, 0:256]
        WREC = big[:, 10272:11296].rearrange("p (b j) -> p b j", b=8)
        WING = big[:, 11296:12320].rearrange("p (b j) -> p b j", b=8)
        TMP = big[:, 10272:12320].rearrange("p (b s) -> p b s", b=8)
        RGATE = big[:, 12320:14368].rearrange("p (b s) -> p b s", b=8)
        IGATE = big[:, 14368:16416].rearrange("p (b s) -> p b s", b=8)
        XC = XSf[:, 0:2048].rearrange("p (b s) -> p b s", b=8)
        GELU = XSf[:, 2048:4096].rearrange("p (b s) -> p b s", b=8)
        PX = P2[:, :, RN2:P2W]
        CT = small[:, 384:640]
        SM = big[:, 16416:17440].rearrange("p (h k) -> p h k", h=4)
        PT = big[:, 17440:18464].rearrange("p (t c) -> p t c", t=2)
        PT1 = big[:, 17408:18432].rearrange("p (t c) -> p t c", t=2)
        SM1 = big[:, 16384:17408].rearrange("p (h k) -> p h k", h=4)
        XTE = XT[:, :, :].rearrange("p b (k s) -> p b k s", k=KC)
        HID = big[:, 6144:7168].rearrange("p (b e f s) -> p b e f s", b=2, e=2, f=2)
        SIL = big[:, 7168:7424].rearrange("p (e f s) -> p e f s", e=2, f=2)
        SEL = big[:, 7424:7936].rearrange("p (b t s) -> p b t s", b=2, t=2)
        SELW = big[:, 7936:8448].rearrange("p (b t s) -> p b t s", b=2, t=2)
        SELT = big[:, 8448:8704]
        YS = big[:, 8704:10752]
        PICK = big[:, 10752:10820].rearrange("p (t e) -> p t e", t=2)
        RANK = big[:, 10820:10888].rearrange("p (t e) -> p t e", t=2)
        CW = big[:, 10888:10956].rearrange("p (t e) -> p t e", t=2)
        COMB = CW[:, :, 0:EXPERTS]
        now_rank = big[:, 10956:10964].rearrange("p (t e) -> p t e", t=2)
        now_cw = big[:, 10964:10972].rearrange("p (t e) -> p t e", t=2)
        most, over = big[:, 10972:10973], big[:, 10973:10976]
        rounds = big[:, 10976:10977].bitcast(mybir.dt.int32)
        PIN = big[:, 1024:1536].rearrange("p (t n) -> p t n", t=2)
        PINT = big[:, 1536:2048].rearrange("p (t n) -> p t n", t=2)
        WUP = big[:, 2048:6144].rearrange("p (k n) -> p k n", k=2)

        ss, rms, rstd = small[:, 0:2], small[:, 2:4], small[:, 4:6]
        mx, nmx, rs, es, rden = (small[:, 8 + 4 * j:12 + 4 * j] for j in range(5))
        STATS = small[:, 32:128].rearrange("p (g s) -> p g s", g=16)
        MV = small[:, 128:160].rearrange("p (g s) -> p g s", g=16)
        ORMS, ORSTD = small[:, 160:176], small[:, 176:192]
        hrms = small[:, 192:208].rearrange("p (t h) -> p t h", t=2)
        hrstd = small[:, 208:224].rearrange("p (t h) -> p t h", t=2)
        SPV = small[:, 224:248]
        SPZ, SPS, SPQ, SPA = (small[:, 248 + 24 * j:272 + 24 * j] for j in range(4))
        CUM = small[:, 344:360].rearrange("p (t h) -> p t h", t=2)
        LF = small[:, 360:376].rearrange("p (t h) -> p t h", t=2)
        lru_neg, lru_pos = small[:, 376:384], small[:, 0:8]
        gate_sum = small[:, 96:112].rearrange("p (t h) -> p t h", t=2)
        dots = small[:, 32:48]
        acts = small[:, 48:64]
        wts = small[:, 64:80]
        RL = small[:, 32:112].rearrange("p (t e) -> p t e", t=2)
        ML = small[:, 112:176].rearrange("p (t e) -> p t e", t=2)
        TOPV = small[:, 176:208].rearrange("p (t g e) -> p t g e", t=2, g=2)
        TOPU = small[:, 208:240].bitcast(u32).rearrange("p (t g e) -> p t g e", t=2, g=2)
        TOPF = small[:, 240:272].rearrange("p (t g e) -> p t g e", t=2, g=2)
        GEXP = small[:, 272:280].rearrange("p (t g) -> p t g", t=2)
        RSC = small[:, 280:296].rearrange("p (t g) -> p t g", t=2)
        HOT32 = small[:, 448:512].rearrange("p (t e) -> p t e", t=2)

        bank = [ctx.enter_context(nc.psum_tensor(f"bank{i}", [P, CH], f32)) for i in range(8)]

        w_loaded = [sem(f"w_loaded{s}") for s in range(SLOTS)]
        w_used = sem("w_used")
        set_free = sem("set_free")
        x_loaded, c_loaded, g_loaded = sem("x_loaded"), sem("c_loaded"), sem("g_loaded")
        rows_loaded = sem("rows_loaded")
        gt_turned, gt_ready = sem("gt_turned"), sem("gt_ready")
        rms_ready, xs_ready, x_turned = sem("rms_ready"), sem("xs_ready"), sem("x_turned")
        xt_act, xt_dve = sem("xt_act"), sem("xt_dve")
        roped = sem("roped")
        turned, turn_kept = sem("turned"), sem("turn_kept")
        scored, scores_ready, exp_ready, probs_ready = (
            sem(n) for n in ("scored", "scores_ready", "exp_ready", "probs_ready"))
        probs_turned, probs_kept, attended, attn_kept = (
            sem(n) for n in ("probs_turned", "probs_kept", "attended", "attn_kept"))
        ret_inner, inner_ready, state_ready, ret_out, ret_stats, ret_kept = (
            sem(n) for n in ("ret_inner", "inner_ready", "state_ready", "ret_out", "ret_stats", "ret_kept"))
        var_ready, ret_rms, ret_ready = sem("var_ready"), sem("ret_rms"), sem("ret_ready")
        merged = sem("merged")
        keys_loaded, grow_loaded, hn_ready = sem("keys_loaded"), sem("grow_loaded"), sem("hn_ready")
        keys_turned, keys_kept, peer_scored, s_kept = (
            sem(n) for n in ("keys_turned", "keys_kept", "peer_scored", "s_kept"))
        best_ready, gate_exp, idx_ready = sem("best_ready"), sem("gate_exp"), sem("idx_ready")
        down_in = [sem(f"down_in{b}") for b in range(4)]
        up_in = [sem(f"up_in{b}") for b in range(4)]
        gathers = sem("gathers")
        dotted, weight_ready, added = sem("dotted"), sem("weight_ready"), sem("added")
        peer_done, fin_rms, x2_ready = sem("peer_done"), sem("fin_rms"), sem("x2_ready")
        lru_loaded = sem("lru_loaded")
        fl_done, sp_in, sp_exp, sp_done, cum_done, cum_kept = (
            sem(n) for n in ("fl_done", "sp_in", "sp_exp", "sp_done", "cum_done", "cum_kept"))
        conv_ready, lru_mm, gates_ready, decay_ready, gap_ready, gap_root, rnn_ready = (
            sem(n) for n in ("conv_ready", "lru_mm", "gates_ready", "decay_ready", "gap_ready",
                             "gap_root", "rnn_ready"))
        hsq_ready, hrms_ready, qk_ready = sem("hsq_ready"), sem("hrms_ready"), sem("qk_ready")
        routed, route_in, route_exp, comb_ready = (
            sem(n) for n in ("routed", "route_in", "route_exp", "comb_ready"))
        ranked, rounds_ready, sel_ready, xte_mm, xte_kept = (
            sem(n) for n in ("ranked", "rounds_ready", "sel_ready", "xte_mm", "xte_kept"))
        silu_ready, hid_ready, selt_mm, selt_kept, y_mm, y_act, y_dve = (
            sem(n) for n in ("silu_ready", "hid_ready", "selt_mm", "selt_kept", "y_mm", "y_act", "y_dve"))
        scat_mm, scat_added, moe_done = (sem(n) for n in ("scat_mm", "scat_added", "moe_done"))
        ple_loaded, up_done, out_ready, out_stored = (
            sem(n) for n in ("ple_loaded", "up_done", "out_ready", "out_stored"))

        block = ctx.enter_context(nc.Block())

        def unit_count(u):
            return 16 * (u // SLOTS + 1)

        def slot(u, n):
            return W[:, u % SLOTS, :].rearrange("p (k n) -> p k n", n=n)

        def group(n):
            return 4 * ((n // 2) % 2), n % 2, P * (n % 2 + 1)

        def att(n):
            return (P1, QA, KA, VA, SM1, PT1) if n < 4 else (P2, Q2, K2, V2, SM, PT)

        @block.sync
        def _(sp):
            def load(u, src, i=None, per=0, n=CH):
                if u >= SLOTS:
                    sp.wait_ge(w_used, i * per + (u - SLOTS + 1) if i is not None else u - SLOTS + 1)
                sp.dma_start(slot(u, n), src).then_inc(w_loaded[u % SLOTS], 16)

            def rows(w, k0, k, c, n=CH):
                return w.rearrange("(k p) n -> p k n", p=P)[:, k0:k0 + k, ds(c, n)]

            w_in, w_ab, w_rb, w_out = A["w_in"][0], A["w_attn_branch"][0], A["w_ret_branch"][0], A["w_out"][0]
            sp.dma_start(H[:, :, :], A["x"][0].rearrange("(t p) n -> p t n", p=P)).then_inc(x_loaded, 16)
            sp.dma_start(C[:, :], consts).then_inc(c_loaded, 16)
            sp.wait_ge(g_loaded, 10 * 16)
            for u in range(4):
                load(u, rows(w_in, 8 * (u % 2), 8, CH * (u // 2)))
            with sp.Fori(0, 6) as i:
                for j in range(4):
                    load(UA + 4 + j, rows(w_in, 8 * (j % 2), 8, i * (2 * CH) + (2 + j // 2) * CH), i, 4)
            for u in (28, 29):
                load(u, rows(w_in, 8 * (u % 2), 8, CH * 14))
            for n in range(4):
                u = UB + 7 * n
                for j in range(2):
                    load(u + j, rows(w_in, 8 * j, 8, GATE_A + CH * n))
                for j in range(2):
                    load(u + 2 + j, rows(w_in, 8 * j, 8, GATE_R + CH * n))
                load(u + 4, rows(w_ab, 0, 8, CH * n))
                for j in range(2):
                    load(u + 5 + j, rows(w_rb, 8 * j, 8, CH * n))

            def load_square(u0, w):
                with sp.Fori(0, 2) as i:
                    for j in range(4):
                        load(u0 + j, rows(w, 8 * (j % 2), 8, i * (2 * CH) + (j // 2) * CH), i, 4)

            load_square(UC, w_out)
            load_square(UD, A["w_peer_query"][0])
            sp.wait_ge(w_used, UD)
            sp.dma_start(KEYS, A["peer_sub_keys"][0].rearrange("q h n d -> n (q h) d")).then_inc(keys_loaded, 16)
            sp.dma_start(GROW, A["ffn_norm"].to_broadcast([P, D])).then_inc(grow_loaded, 16)
            sp.wait_ge(hn_ready, 2)
            sp.dma_start(GROW, A["final_norm"].unsqueeze(0).to_broadcast([P, D])).then_inc(grow_loaded, 16)
            sp.wait_ge(peer_done, 1)
            w2 = A["w_in_2"][0]
            col = {"q": Q2, "k": K2, "v": V2, "rx": W2_RX, "rg": W2_RG}
            sp.dma_start(WREC, A["w_rec_gate_2"][0].rearrange("b i j -> i b j")).then_inc(lru_loaded, 16)
            sp.dma_start(WING, A["w_in_gate_2"][0].rearrange("b i j -> i b j")).then_inc(lru_loaded, 16)
            for c, (kind, n) in enumerate(CHUNK_E):
                for j in range(2):
                    load(UE + 2 * c + j, rows(w2, 8 * j, 8, col[kind] + CH * n))
            load_square(UF, A["w_out_2"][0])
            sp.wait_ge(w_used, UG)
            sp.dma_start(PIN, A["p_2"][0, 0].rearrange("(t p) n -> p t n", p=P)).then_inc(ple_loaded, 16)
            sp.dma_start(WUP, A["w_ple_up_2"][0].rearrange("(k p) n -> p k n", p=P)).then_inc(ple_loaded, 16)
            wg = A["w_expert_gate_2"].rearrange("o e (k p) n -> p (o e k) n", p=P)
            wu = A["w_expert_up_2"].rearrange("o e (k p) n -> p (o e k) n", p=P)
            wd = A["w_expert_down_2"].rearrange("o e (k p) n -> p (o e k) n", p=P)
            sp.wait_ge(rounds_ready, 1)
            n_rounds = sp.value_load(rounds[0:1, 0:1], min_val=1, max_val=MAX_ROUNDS)
            with sp.Fori(0, n_rounds) as r, sp.Fori(0, PAIRS // 2) as i:
                for j in range(2 * PAIR_UNITS):
                    e, kind = 2 * (j // PAIR_UNITS), j % PAIR_UNITS
                    u = UG + j
                    sp.wait_ge(w_used, r * ROUND_UNITS + i * (2 * PAIR_UNITS) + (u - SLOTS + 1))
                    if kind < 4:
                        src = (wu if kind % 2 else wg)[:, ds(i * (4 * KC) + (e + kind // 2) * KC, KC), :]
                    else:
                        src = wd[:, ds(i * 8 + (e + kind - 4) * 2, 2), :]
                    sp.dma_start(slot(u, DE if kind < 4 else D), src).then_inc(w_loaded[u % SLOTS], 16)
            w_pg = A["w_ple_gate_2"][0]
            for j in range(8):
                u = UG + j
                sp.wait_ge(w_used, n_rounds * ROUND_UNITS + (u - SLOTS + 1))
                sp.dma_start(slot(u, CH), rows(w_pg, 8 * (j % 2), 8, CH * (j // 2))).then_inc(w_loaded[u % SLOTS], 16)
            out_t = out[0].rearrange("(t p) n -> p t n", p=P)
            for n in range(4):
                sp.wait_ge(out_ready, n + 1)
                sp.dma_start(out_t[:, :, CH * n:CH * (n + 1)], H[:, :, CH * n:CH * (n + 1)]).then_inc(out_stored, 16)
            sp.wait_ge(out_stored, 64)

        @block.gpsimd
        def _(pool):
            r = 0
            for name in ("attn_norm", "ffn_norm", "mix_norm_2", "ffn_norm_2", "ple_norm_2"):
                pool.dma_start(gains_raw[r:r + 16, 0, :], A[name].rearrange("o (k p) -> (o k) p", p=P)).then_inc(g_loaded, 16)
                r += 16
            pool.dma_start(gains_raw[0:32, 1, :], A["conv_w_2"].rearrange("o c (k p) -> (o c k) p", p=P)).then_inc(g_loaded, 16)
            r = 32
            for name in ("conv_b_2", "b_rec_gate_2", "b_in_gate_2", "lru_lambda_2"):
                pool.dma_start(gains_raw[r:r + 8, 1, :], A[name].rearrange("o (k p) -> (o k) p", p=P)).then_inc(g_loaded, 16)
                r += 8
            pool.dma_start(rowc[:, 0:8], A["attn_sinks"].to_broadcast([P, 8])).then_inc(rows_loaded, 16)
            pool.dma_start(rowc[:, 8:16], A["b_forget_2"].to_broadcast([P, 8])).then_inc(rows_loaded, 16)
            pool.dma_start(rowc[:, 16:144], A["q_norm_2"].to_broadcast([P, P])).then_inc(rows_loaded, 16)
            pool.dma_start(rowc[:, 144:272], A["k_norm_2"].to_broadcast([P, P])).then_inc(rows_loaded, 16)
            pool.dma_start(WR[:, :, 0:4], A["w_router_group_2"][0].rearrange("(k p) n -> p k n", p=P)).then_inc(rows_loaded, 16)
            pool.dma_start(WR[:, :, 4:36], A["w_router_expert_2"][0].rearrange("(k p) n -> p k n", p=P)).then_inc(rows_loaded, 16)
            pool.dma_start(WF[:, :, :], A["w_in_2"][0].rearrange("(k p) n -> p k n", p=P)[:, :, W2_F:W2_F + 8]).then_inc(rows_loaded, 16)
            down_t, up_t = A["peer_expert_down"][0], A["peer_expert_up"][0]
            pool.wait_ge(w_used, UE)
            for g in range(2 * T2):
                t = g // 2
                pool.wait_ge(idx_ready, g + 1)
                with pool.Fori(2 * (g % 2), 2 * (g % 2) + 2) as i:
                    for j in range(2 * TOPK):
                        idx = idx_cur[:, j // TOPK, :]
                        at = TOPK * HEADS * t + j
                        if j % TOPK == 0:
                            pool.tensor_copy(idx, idx_all[:, t, ds(i * (2 * TOPK) + j, TOPK)])
                            pool.drain()
                        row = bass.IndirectOffsetOnAxis(idx[:, j % TOPK:j % TOPK + 1], 0)
                        pool.wait_ge(dotted, i * (2 * TOPK) + (at + 1))
                        pool.sem_inc(gathers, 1)
                        pool.indirect_dma_start(W[:, j % 4 // 2, (j % 2) * D:(j % 2 + 1) * D],
                                                None, down_t, row).then_inc(down_in[j % 4], 16)
                        pool.wait_ge(added, i * (2 * TOPK) + (at + 1))
                        pool.sem_inc(gathers, 1)
                        pool.indirect_dma_start(W[:, 2 + j % 4 // 2, (j % 2) * D:(j % 2 + 1) * D],
                                                None, up_t, row).then_inc(up_in[j % 4], 16)

        @block.tensor
        def _(pe):
            turns = 0

            def xt(k, t):
                return XT[:, t, k * P:(k + 1) * P]

            def turn_norm(j):
                pe.wait_ge(xs_ready, 2 * (j + 1))
                for k in range(KC):
                    if k >= 4:
                        pe.wait_ge(xt_dve if k % 2 else xt_act, 8 * j + (k - 4) // 2 + 1)
                    for t in range(T2):
                        last = pe.transpose(bank[4 + k % 4][:, t * P:(t + 1) * P], XS[:, t, k * P:(k + 1) * P], ident)
                    last.then_inc(x_turned, 1)
                pe.wait_ge(xt_act, 8 * (j + 1))
                pe.wait_ge(xt_dve, 8 * (j + 1))

            def wait_unit(u, i=None, per=0):
                pe.wait_ge(w_loaded[u % SLOTS], i * (16 * per // SLOTS) + unit_count(u) if i is not None else unit_count(u))

            def wait_set(q, i=None):
                pe.wait_ge(set_free, i * 4 + (2 * q + 2) if i is not None else 2 * q + 2)

            def unit_natural(u, ps, lhs, k0, kn, first, last_unit, i=None, per=0):
                wait_unit(u, i, per)
                w = slot(u, CH)
                for t in range(T2):
                    for k in range(kn):
                        mm = pe.matmul(ps[t][:, :], lhs(k0 + k, t), w[:, k, :],
                                       start=first and k == 0, stop=last_unit and k == kn - 1)
                mm.then_inc(w_used, 1)

            def chunk_turned(u, ps, i=None, per=0):
                wait_unit(u, i, per)
                wait_unit(u + 1, i, per)
                for b in range(4):
                    o = ps[b // 2][:, (b % 2) * 256:(b % 2 + 1) * 256].rearrange("p (t s) -> p t s", t=2)
                    for k in range(KC):
                        mm = pe.matmul(o, slot(u + k // 8, CH)[:, k % 8, b * P:(b + 1) * P],
                                       XT[:, :, k * P:(k + 1) * P], start=k == 0, stop=k == KC - 1)
                mm.then_inc(w_used, 2)

            def square(u0, q0, lhs):
                with pe.Fori(0, 2) as i:
                    for c in range(2):
                        q, u = q0 + c, u0 + 2 * c
                        wait_set(q, i)
                        ps = bank[2 * (q % 2):2 * (q % 2) + 2]
                        for j in range(2):
                            unit_natural(u + j, ps, lhs, 8 * j, 8, j == 0, j == 1, i, 4)

            def turn(buf, src, n):
                nonlocal turns
                pe.wait_ge(attn_kept, scored_so_far) if scored_so_far else None
                for c in range(0, n, 256):
                    if turns >= 4:
                        pe.wait_ge(turn_kept, turns - 3)
                    for t in range(T2):
                        for b in range(2):
                            at = src + c + b * P
                            last = pe.transpose(bank[4 + turns % 4][:, (2 * t + b) * P:(2 * t + b + 1) * P],
                                                buf[:, t, at:at + P], ident)
                    last.then_inc(turned, 1)
                    turns += 1

            scored_so_far = 0

            def scores(n):
                nonlocal scored_so_far
                buf, cq, ck, _, _, _ = att(n)
                h0, t, nk = group(n)
                pe.wait_ge(turn_kept, turns)
                if n:
                    pe.wait_ge(attn_kept, n)
                if n >= 4:
                    pe.wait_ge(cum_kept, 2)
                for hh in range(4):
                    h = h0 + hh
                    o = bank[4 + hh // 2][:, (hh % 2) * 256:(hh % 2) * 256 + nk]
                    kcol = ck + (h0 // 4 * P if n < 4 else h * P)
                    keys = buf[:, 0:2, kcol:kcol + P] if nk > P else buf[:, 0, kcol:kcol + P]
                    mm = pe.matmul(o.rearrange("p (t s) -> p t s", s=P) if nk > P else o,
                                   buf[:, t, cq + h * P:cq + (h + 1) * P], keys, start=True, stop=n < 4)
                    if n >= 4:
                        mm = pe.matmul(o, const("sel")[:, h * P:(h + 1) * P], CT[:, 0:nk], start=False, stop=True)
                mm.then_inc(scored, 1)
                scored_so_far = n + 1

            def turn_probs(n):
                _, _, _, _, sm, _ = att(n)
                h0, t, nk = group(n)
                pe.wait_ge(probs_ready, n + 1)
                for kt in range(nk // P):
                    for hh in range(4):
                        last = pe.transpose(bank[6 + kt][:, hh * P:(hh + 1) * P], sm[:, hh, kt * P:(kt + 1) * P], ident)
                last.then_inc(probs_turned, 1)

            def values(n):
                buf, _, _, cv, _, pt = att(n)
                h0, t, nk = group(n)
                pe.wait_ge(probs_kept, n + 1)
                nt = nk // P
                if n < 4:
                    v = cv + h0 // 4 * P
                    for kt in range(nt):
                        mm = pe.matmul(bank[4][:, :], buf[:, kt, v:v + P], pt[:, kt, :], start=kt == 0, stop=kt == nt - 1)
                else:
                    for hh in range(4):
                        v = cv + (h0 + hh) * P
                        for kt in range(nt):
                            mm = pe.matmul(bank[4][:, hh * P:(hh + 1) * P], buf[:, kt, v:v + P],
                                           pt[:, kt, hh * P:(hh + 1) * P], start=kt == 0, stop=kt == nt - 1)
                mm.then_inc(attended, 1)

            def retention(i):
                if i == 0:
                    pe.wait_ge(turn_kept, turns)
                    pe.wait_ge(attn_kept, 4)
                if i < HEADS:
                    if i:
                        pe.wait_ge(inner_ready, i)
                        pe.wait_ge(state_ready, i)
                    for t in range(T2):
                        mm = pe.matmul(bank[4][:, t * P:(t + 1) * P], P1[:, t, KR + i * P:KR + (i + 1) * P],
                                       P1[:, t, QR + i * P:QR + (i + 1) * P], start=True, stop=True)
                    mm = pe.matmul(bank[5][:, 0:256], KDEC[:, i, :], P1[:, 0, VR + 256 * i:VR + 256 * (i + 1)],
                                   start=True, stop=True)
                    mm.then_inc(ret_inner, 1)
                if i:
                    h = i - 1
                    pe.wait_ge(inner_ready, h + 1)
                    pe.wait_ge(state_ready, h + 1)
                    if h >= 2:
                        pe.wait_ge(ret_stats, h - 1)
                        pe.wait_ge(ret_kept, h - 1)
                    o = bank[6 + h % 2]
                    v = VR + 256 * h
                    pe.matmul(o[:, 0:256], IN[:, h % 2, 0, :], P1[:, 0, v:v + 256], start=True, stop=True)
                    pe.matmul(o[:, 256:512], IN[:, h % 2, 1, :], P1[:, 1, v:v + 256], start=True, stop=False)
                    pe.matmul(o[:, 256:512], P1[:, 1, QR + h * P:QR + (h + 1) * P], KV[:, h % 2, :],
                              start=False, stop=True).then_inc(ret_out, 1)

            pe.wait_ge(c_loaded, 16)
            pe.wait_ge(g_loaded, 10 * 16)
            pe.transpose(bank[4][:, 0:80], gains_raw[0:80, 0, :], ident[0:80, 0:80])
            pe.transpose(bank[5][:, 0:64], gains_raw[0:64, 1, :], ident[0:64, 0:64]).then_inc(gt_turned, 1)
            pe.wait_ge(gt_ready, 2)
            turn_norm(0)

            ready = {QA: (roped, 1), QA + 512: (roped, 1), KA: (roped, 2), QR: (roped, 3), QR + 512: (roped, 3),
                     KR: (roped, 4), KR + 512: (roped, 4), **{GR + 512 * j: (ret_ready, 1) for j in range(4)},
                     **{VR + 512 * j: (merged, j + 1) for j in range(4)}}
            for u in range(UB + 28):
                if u < UB:
                    if u % 2 == 0:
                        wait_set(u // 2)
                    q = u // 2
                    unit_natural(u, bank[2 * (q % 2):2 * (q % 2) + 2], xt, 8 * (u % 2), 8, u % 2 == 0, u % 2 == 1)
                else:
                    n, j = (u - UB) // 7, (u - UB) % 7
                    if j < 4:
                        q = QCB + 2 * n + j // 2
                        if j % 2 == 0:
                            wait_set(q)
                        unit_natural(u, bank[2 * (q % 2):2 * (q % 2) + 2], xt, 8 * (j % 2), 8, j % 2 == 0, j % 2 == 1)
                    elif j == 4:
                        pe.wait_ge(turn_kept, turns)
                        pe.wait_ge(ret_stats, HEADS)
                        pe.wait_ge(ret_kept, HEADS)
                        if n:
                            pe.wait_ge(merged, n)
                        unit_natural(u, bank[4:6], lambda k, t: P1[:, t, QA + k * P:QA + (k + 1) * P], 0, 8, True, True)
                    else:
                        unit_natural(u, bank[6:8], lambda k, t: P1[:, t, QR + k * P:QR + (k + 1) * P],
                                     8 * (j - 5), 8, j == 5, j == 6)
                for step in AFTER1.get(u, ()):
                    if step[0] == "tr":
                        pe.wait_ge(*ready[step[1]])
                        turn(P1, step[1], step[3])
                    elif step[0] == "S":
                        scores(step[1])
                    elif step[0] == "T":
                        turn_probs(step[1])
                    elif step[0] == "V":
                        values(step[1])
                    elif step[0] == "R":
                        retention(step[1])

            pe.wait_ge(turn_kept, turns)
            square(UC, QCC, lambda k, t: P1[:, t, GR + k * P:GR + (k + 1) * P])

            turn_norm(1)
            with pe.Fori(0, 2) as i:
                for c in range(2):
                    q, u = QCD + c, UD + 2 * c
                    wait_set(q, i)
                    chunk_turned(u, bank[2 * (q % 2):2 * (q % 2) + 2], i, 4)
            pe.wait_ge(keys_loaded, 16)
            for b in range(16):
                last = pe.transpose(bank[4 + b // 4][:, (b % 4) * P:(b % 4 + 1) * P], KEYS[:, b, :], ident)
            last.then_inc(keys_turned, 1)
            pe.wait_ge(keys_kept, 4)
            pe.wait_ge(set_free, CREDITS + 2 * (QCD + 4))
            for r in range(8):
                t, b0 = r // 4, 4 * (r % 4)
                if r >= 4:
                    pe.wait_ge(s_kept, r - 3)
                for b in range(b0, b0 + 4):
                    mm = pe.matmul(bank[4 + r % 4][:, (b % 4) * P:(b % 4 + 1) * P], QT[:, t, b * P:(b + 1) * P],
                                   KT[:, (b % 2) * 8 + b // 2, :], start=True, stop=True)
                mm.then_inc(peer_scored, 1)

            pe.wait_ge(rows_loaded, 7 * 16)
            turn_norm(2)
            ready2 = {Q2: 1, Q2 + 512: 1, K2: 2, K2 + 512: 2}
            for c, (kind, n) in enumerate(CHUNK_E):
                q = QCE + c
                ps = bank[2 * (q % 2):2 * (q % 2) + 2]
                for half in range(2):
                    u = UE + 2 * c + half
                    if half == 0:
                        wait_set(q)
                    if kind in ("q", "k", "v"):
                        unit_natural(u, ps, xt, 8 * half, 8, half == 0, half == 1)
                    elif half == 1:
                        chunk_turned(u - 1, ps)
                    for step in AFTER2.get(2 * c + half, ()):
                        if step[0] == "tr":
                            pe.wait_ge(qk_ready, ready2[step[1]])
                            turn(P2, step[1], step[3])
                        elif step[0] == "S":
                            scores(step[1])
                        elif step[0] == "T":
                            turn_probs(step[1])
                        elif step[0] == "V":
                            values(step[1])
                        elif step[0] == "FL":
                            for t in range(T2):
                                for k in range(KC):
                                    mm = pe.matmul(bank[4][:, 8 * t:8 * t + 8], xt(k, t), WF[:, k, :],
                                                   start=k == 0, stop=k == KC - 1)
                            mm.then_inc(fl_done, 1)
                        elif step[0] == "LG":
                            if step[1] == 0:
                                pe.wait_ge(conv_ready, 1)
                                pe.wait_ge(lru_loaded, 32)
                                pe.wait_ge(sp_in, 1)
                            else:
                                pe.wait_ge(gates_ready, 8)
                            for b in range(8):
                                mm = pe.matmul(bank[4 + b // 2][:, (b % 2) * 256:(b % 2 + 1) * 256],
                                               (WING if step[1] else WREC)[:, b, :], XC[:, b, :], start=True, stop=True)
                            mm.then_inc(lru_mm, 1)
                        elif step[0] == "FC":
                            pe.wait_ge(sp_done, 1)
                            pe.wait_ge(gates_ready, 16)
                            tri = const("tri")
                            pe.matmul(bank[4][:, 0:8], tri[:, 0:P], LF[:, 0, :], start=True, stop=True)
                            pe.matmul(bank[4][:, 8:16], tri[:, P:2 * P], LF[:, 0, :], start=True, stop=False)
                            pe.matmul(bank[4][:, 8:16], tri[:, 0:P], LF[:, 1, :], start=False, stop=True)
                            pe.matmul(bank[5][0:8, 0:P], LF[:, 0, :], tri[:, 0:P], start=True, stop=True)
                            pe.matmul(bank[5][0:8, P:2 * P], LF[:, 0, :], tri[:, P:2 * P], start=True, stop=False)
                            pe.matmul(bank[5][0:8, P:2 * P], LF[:, 1, :], tri[:, 0:P],
                                      start=False, stop=True).then_inc(cum_done, 1)
            pe.wait_ge(attn_kept, 8)
            pe.wait_ge(rnn_ready, 1)
            square(UF, QCF, lambda k, t: P2[:, t, k * P:(k + 1) * P] if k < 8 else
                   P2[:, t, RN2 + (k - 8) * P:RN2 + (k - 7) * P])

            turn_norm(3)
            for t in range(T2):
                for k in range(KC):
                    mm = pe.matmul(bank[4][:, 64 * t:64 * t + 36], xt(k, t), WR[:, k, :], start=k == 0, stop=k == KC - 1)
            mm.then_inc(routed, 1)
            pe.wait_ge(comb_ready, 1)
            tri = const("tri")
            for o, a in ((0, 0), (EXPERTS, P)):
                mm = pe.matmul(bank[5][:, o:o + EXPERTS], tri[:, a:a + P], PICK[:, 0, 0:EXPERTS], start=True, stop=o == 0)
            pe.matmul(bank[5][:, EXPERTS:2 * EXPERTS], tri[:, 0:P], PICK[:, 1, 0:EXPERTS], start=False, stop=True)
            for t in range(T2):
                mm = pe.matmul(bank[5][:, 2 * EXPERTS:3 * EXPERTS], tri[:, P:2 * P], PICK[:, t, 0:EXPERTS],
                               start=t == 0, stop=t == 1)
            mm.then_inc(ranked, 1)
            pe.wait_ge(set_free, CREDITS + 2 * QCH)
            pe.wait_ge(rounds_ready, 1)
            n_rounds = pe.value_load(rounds[0:1, 0:1], min_val=1, max_val=MAX_ROUNDS)

            def pick_tokens(buf, first_wait, kept):
                for b in range(4):
                    if b == 0:
                        pe.wait_ge(scat_added, first_wait)
                    if b >= 2:
                        pe.wait_ge(xte_kept, kept + (b - 1))
                    for k in range(4):
                        for t in range(T2):
                            c = (4 * b + k) * P
                            mm = pe.matmul(bank[b % 2][:, k * P:(k + 1) * P], XS[:, t, c:c + P], SEL[:, buf, t, :],
                                           start=t == 0, stop=t == 1)
                    mm.then_inc(xte_mm, 1)

            with pe.Fori(0, n_rounds) as r:
                pe.wait_ge(sel_ready, r * (PAIRS + 1) + 1)
                pick_tokens(0, r * (8 * PAIRS) + 8, r * (4 * PAIRS + 4))
                with pe.Fori(0, PAIRS // 2) as i:
                    for p in range(2):
                        u0 = UG + PAIR_UNITS * p

                        def unit(j):
                            u = u0 + j
                            pe.wait_ge(w_loaded[u % SLOTS], r * (16 * ROUND_UNITS // SLOTS) +
                                       i * (16 * 2 * PAIR_UNITS // SLOTS) + unit_count(u))
                            return slot(u, DE if j < 4 else D)

                        pe.wait_ge(xte_kept, r * (4 * PAIRS + 4) + i * 8 + 4 * (p + 1))
                        for e in range(2):
                            pe.wait_ge(hid_ready, r * EXPERTS + i * 4 + (2 * p + e + 1))
                            if e:
                                pe.wait_ge(selt_kept, r * PAIRS + i * 2 + (p + 1))
                            for j in range(2):
                                w = unit(2 * e + j)
                                for f in range(2):
                                    o = bank[2 + e][:, (2 * j + f) * CAP:(2 * j + f + 1) * CAP]
                                    for k in range(KC):
                                        mm = pe.matmul(o, w[:, k, f * P:(f + 1) * P], XTE[:, p, k, e * CAP:(e + 1) * CAP],
                                                       start=k == 0, stop=k == KC - 1)
                                mm.then_inc(w_used, 1)
                        pe.wait_ge(sel_ready, r * (PAIRS + 1) + i * 2 + (p + 2))
                        pick_tokens(1 - p, r * (8 * PAIRS) + i * 16 + (8 * p + 8), r * (4 * PAIRS + 4) + i * 8 + 4 * (p + 1))
                        pe.wait_ge(hid_ready, r * EXPERTS + i * 4 + (2 * p + 4))
                        for t in range(T2):
                            last = pe.transpose(bank[3][:, 256 + t * P:256 + (t + 1) * P], SELW[:, p, t, :], ident)
                        last.then_inc(selt_mm, 1)
                        for e in range(2):
                            w = unit(4 + e)
                            for n in range(4):
                                if e == 0:
                                    pe.wait_ge(y_dve if n % 2 else y_act, r * (2 * PAIRS) + i * 4 + (2 * p + n // 2 + 1))
                                for f in range(2):
                                    mm = pe.matmul(bank[4 + n][:, :], HID[:, p, e, f, :], w[:, f, n * CH:(n + 1) * CH],
                                                   start=e == 0 and f == 0, stop=e == 1 and f == 1)
                                if n == 3:
                                    mm.then_inc(w_used, 1)
                                elif e:
                                    mm.then_inc(y_mm, 1)
                        pe.wait_ge(selt_kept, r * PAIRS + i * 2 + (p + 2))
                        pe.wait_ge(xte_kept, r * (4 * PAIRS + 4) + i * 8 + (4 * p + 8))
                        for n in range(4):
                            pe.wait_ge(y_dve if n % 2 else y_act, r * (2 * PAIRS) + i * 4 + (2 * p + n // 2 + 3))
                            for t in range(T2):
                                if n:
                                    pe.wait_ge(scat_added, r * (8 * PAIRS) + i * 16 + (8 * p + 2 * n + t + 7))
                                pe.matmul(bank[t][:, :], SELT[:, t * P:(t + 1) * P], YS[:, n * CH:(n + 1) * CH],
                                          start=True, stop=True).then_inc(scat_mm, 1)

            turn_norm(4)
            pe.wait_ge(ple_loaded, 32)
            turn(PIN, 0, 256)
            pe.wait_ge(turn_kept, turns)
            for n in range(4):
                q = QCH + n
                if n >= 2:
                    pe.wait_ge(out_ready, n - 1)
                for t in range(T2):
                    for k in range(2):
                        mm = pe.matmul(bank[4 + 2 * (n % 2) + t][:, :], PINT[:, t, k * P:(k + 1) * P],
                                       WUP[:, k, n * CH:(n + 1) * CH], start=k == 0, stop=k == 1)
                mm.then_inc(up_done, 1)
                wait_set(q)
                for j in range(2):
                    u = UG + 2 * n + j
                    pe.wait_ge(w_loaded[u % SLOTS], n_rounds * (16 * ROUND_UNITS // SLOTS) + unit_count(u))
                    for t in range(T2):
                        for k in range(8):
                            mm = pe.matmul(bank[2 * (q % 2) + t][:, :], xt(8 * j + k, t), slot(u, CH)[:, k, :],
                                           start=j == 0 and k == 0, stop=j == 1 and k == 7)
                    mm.then_inc(w_used, 1)

        @block.scalar
        def _(act):
            def root_mean_square(ready, value, done):
                act.wait_ge(ready, value)
                for t in range(T2):
                    act.activation(XS[:, t, :], H[:, t, :], ACT.Square, accum_out=ss[:, t:t + 1])
                act.drain()
                act.activation(rms, ss, ACT.Sqrt, scale=1.0 / D, bias=eps).then_inc(done, 1)

            def keep_norm(j):
                for k in range(0, KC, 2):
                    act.wait_ge(x_turned, KC * j + k + 1)
                    act.activation(XT[:, :, k * P:(k + 1) * P], bank[4 + k % 4][:, 0:256].rearrange("p (t s) -> p t s", t=2),
                                   ACT.Copy, scale=GT[:, 16 * j + k:16 * j + k + 1]).then_inc(xt_act, 1)

            turns = 0

            def keep_turned(buf, dst, n):
                nonlocal turns
                for c in range(0, n, 256):
                    act.wait_ge(turned, turns + 1)
                    act.activation(buf[:, :, dst + c:dst + c + 256],
                                   bank[4 + turns % 4][:, :].rearrange("p (t s) -> p t s", t=2), ACT.Copy).then_inc(turn_kept, 1)
                    turns += 1

            def exps(n):
                _, _, _, _, sm, _ = att(n)
                _, _, nk = group(n)
                act.wait_ge(scores_ready, n + 1)
                for hh in range(4):
                    act.activation(sm[:, hh, 0:nk], sm[:, hh, 0:nk], ACT.Exp, bias=nmx[:, hh:hh + 1],
                                   accum_out=rs[:, hh:hh + 1]).then_inc(exp_ready, 1)
                if n < 4:
                    act.activation(es, es, ACT.Exp).then_inc(exp_ready, 1)
                else:
                    act.activation(es, nmx, ACT.Copy).then_inc(exp_ready, 1)

            def keep_probs(n):
                _, _, _, _, _, pt = att(n)
                _, _, nk = group(n)
                act.wait_ge(probs_turned, n + 1)
                for kt in range(nk // P):
                    last = act.activation(pt[:, kt, :], bank[6 + kt][:, :], ACT.Copy)
                    if kt == nk // P - 1:
                        last.then_inc(probs_kept, 1)

            def keep_attended(n):
                buf, cq, _, _, _, _ = att(n)
                h0, t, _ = group(n)
                act.wait_ge(attended, n + 1)
                act.activation(buf[:, t, cq + h0 * P:cq + h0 * P + CH], bank[4][:, :], ACT.Copy).then_inc(attn_kept, 1)

            act.wait_ge(c_loaded, 16)
            root_mean_square(x_loaded, 16, rms_ready)
            act.wait_ge(gt_ready, 2)
            keep_norm(0)
            for u in range(UB + 28):
                if u < UB and u % 2:
                    c = u // 2
                    act.wait_ge(w_used, u + 1)
                    for t in range(T2):
                        act.activation(P1[:, t, c * CH:(c + 1) * CH], bank[2 * (c % 2) + t][:, :],
                                       ACT.Silu if c * CH >= GR else ACT.Copy).then_inc(set_free, 1)
                for step in AFTER1.get(u, ()):
                    if step[0] == "tr":
                        keep_turned(P1, step[2], step[3])
                    elif step[0] == "S":
                        exps(step[1])
                    elif step[0] == "T":
                        keep_probs(step[1])
                    elif step[0] == "V":
                        keep_attended(step[1])
                    elif step[0] == "R":
                        i = step[1]
                        if i < HEADS:
                            act.wait_ge(ret_inner, i + 1)
                            act.activation(KV[:, i % 2, :], bank[5][:, 0:256], ACT.Copy).then_inc(state_ready, 1)
                        if i:
                            act.wait_ge(ret_stats, i)
                            act.activation(P1[:, :, VR + 256 * (i - 1):VR + 256 * i],
                                           bank[6 + (i - 1) % 2][:, :].rearrange("p (t s) -> p t s", t=2),
                                           ACT.Copy).then_inc(ret_kept, 1)
                    elif step[0] == "rnorm":
                        act.wait_ge(var_ready, 1)
                        act.activation(ORMS, MV[:, :, 1], ACT.Sqrt, bias=eps).then_inc(ret_rms, 1)
                    elif step[0] == "gate":
                        _, n, which = step
                        act.wait_ge(w_used, u + 1)
                        if n:
                            act.wait_ge(merged, n)
                        q = QCB + 2 * n + which
                        for t in range(T2):
                            act.activation(XSf[:, (2 * which + t) * CH:(2 * which + t + 1) * CH],
                                           bank[2 * (q % 2) + t][:, :], ACT.Sigmoid).then_inc(set_free, 1)

            root_mean_square(set_free, CREDITS + 2 * QCD, rms_ready)
            keep_norm(1)
            with act.Fori(0, 2) as i:
                for c in range(2):
                    act.wait_ge(w_used, i * 4 + (UD + 2 * c + 2))
                    for half in range(2):
                        act.activation(QT[:, :, ds(i * (2 * CH) + (c * CH + half * 256), 256)].rearrange("p t (b n) -> p b t n", b=2),
                                       bank[2 * ((QCD + c) % 2) + half][:, :].rearrange("p (b t s) -> p b t s", b=2, t=2),
                                       ACT.Copy).then_inc(set_free, 1)
            act.wait_ge(keys_turned, 1)
            for b in range(4):
                act.activation(KT[:, 4 * b:4 * b + 4, :], bank[4 + b][:, :].rearrange("p (b n) -> p b n", b=4),
                               ACT.Copy).then_inc(keys_kept, 1)
            for r in range(8):
                act.wait_ge(peer_scored, r + 1)
                act.activation(S[:, r // 4, 4 * (r % 4):4 * (r % 4) + 4, :], bank[4 + r % 4][:, :].rearrange("p (b n) -> p b n", b=4),
                               ACT.Copy).then_inc(s_kept, 1)
            gate_cur = small[:, 80:96]

            def gate_exps(g):
                act.wait_ge(best_ready, g + 1)
                gates = gate_all[:, g // 2, (g % 2) * 64:(g % 2 + 1) * 64]
                act.activation(gates, gates, ACT.Exp).then_inc(gate_exp, 1)

            def head_weights(t, first, end):
                with act.Fori(first, end) as h:
                    act.wait_ge(added, h * TOPK + (4 + P * t))
                    act.activation(gate_cur, gate_all[:, t, ds(h * TOPK, TOPK)], ACT.Copy)
                    for j in range(TOPK):
                        act.wait_ge(dotted, h * TOPK + (P * t + j + 5))
                        act.activation(acts[:, j:j + 1], dots[:, j:j + 1], ACT.Gelu)
                        act.drain()
                        act.activation(wts[:, j:j + 1], acts[:, j:j + 1], ACT.Copy,
                                       scale=gate_cur[:, j:j + 1]).then_inc(weight_ready, 1)

            gate_exps(0)
            act.wait_ge(idx_ready, 1)
            for g in range(1, 4):
                head_weights(0, 2 * g - 2, 2 * g)
                gate_exps(g)
                act.wait_ge(idx_ready, g + 1)
            head_weights(0, 6, HEADS)
            head_weights(1, 0, HEADS)
            root_mean_square(peer_done, 1, fin_rms)

            root_mean_square(x2_ready, 2, rms_ready)
            keep_norm(2)
            for c, (kind, n) in enumerate(CHUNK_E):
                q = QCE + c
                for half in range(2):
                    if half:
                        act.wait_ge(w_used, UE + 2 * c + 2)
                        for t in range(T2):
                            ps = bank[2 * (q % 2) + t]
                            pair = ps[:, :].rearrange("p (b s) -> p b s", b=2)
                            if kind == "rx":
                                o = act.activation(RX[:, 4 * n + 2 * t:4 * n + 2 * t + 2, 4:RXP], pair, ACT.Copy)
                            elif kind == "rg":
                                o = act.activation(GELU[:, 4 * n + 2 * t:4 * n + 2 * t + 2, :], pair, ACT.Gelu_apprx_tanh)
                            else:
                                at = {"q": Q2, "k": K2, "v": V2}[kind] + n * CH
                                o = act.activation(P2[:, t, at:at + CH], ps[:, :], ACT.Copy)
                            o.then_inc(set_free, 1)
                    for step in AFTER2.get(2 * c + half, ()):
                        if step[0] == "tr":
                            keep_turned(P2, step[2], step[3])
                        elif step[0] == "S":
                            exps(step[1])
                        elif step[0] == "T":
                            keep_probs(step[1])
                        elif step[0] == "V":
                            keep_attended(step[1])
                        elif step[0] == "FL":
                            act.wait_ge(sp_in, 1)
                            act.activation(SPZ, SPA, ACT.Exp, scale=-1.0).then_inc(sp_exp, 1)
                        elif step[0] == "LG":
                            act.wait_ge(lru_mm, step[1] + 1)
                            for b in range(8):
                                act.activation((IGATE if step[1] else RGATE)[:, b, :],
                                               bank[4 + b // 2][:, (b % 2) * 256:(b % 2 + 1) * 256], ACT.Sigmoid,
                                               bias=(b_ing if step[1] else b_rec)[:, b:b + 1]).then_inc(gates_ready, 1)
                        elif step[0] == "lru":
                            act.wait_ge(sp_done, 1)
                            act.drain()
                            for b in range(8):
                                act.activation(DECAY_A[:, b, :], RGATE[:, b, :], ACT.Exp, scale=lru_neg[:, b:b + 1])
                            act.drain()
                            for b in range(8):
                                act.activation(RGATE[:, b, :], RGATE[:, b, :], ACT.Tanh,
                                               scale=lru_pos[:, b:b + 1]).then_inc(decay_ready, 1)
                            act.wait_ge(gap_ready, 1)
                            act.activation(TMP, TMP, ACT.Sqrt).then_inc(gap_root, 1)
                        elif step[0] == "FC":
                            act.wait_ge(cum_done, 1)
                            act.activation(CT[0:8, :], bank[5][0:8, 0:256], ACT.Copy).then_inc(cum_kept, 1)
                        elif step[0] == "qknorm":
                            act.wait_ge(hsq_ready, step[1] + 1)
                            act.activation(hrms, hrms, ACT.Sqrt, scale=1.0 / HD, bias=eps).then_inc(hrms_ready, 1)

            root_mean_square(set_free, CREDITS + 2 * QCH, rms_ready)
            keep_norm(3)
            act.wait_ge(route_in, 1)
            act.activation(GEXP, GEXP, ACT.Exp)
            act.activation(RSC[:, :, 0:1], RSC[:, :, 0:1], ACT.Exp).then_inc(route_exp, 1)
            act.wait_ge(rounds_ready, 1)
            n_rounds = act.value_load(rounds[0:1, 0:1], min_val=1, max_val=MAX_ROUNDS)

            def keep_tokens(buf, done):
                for b in range(4):
                    act.wait_ge(xte_mm, done + (b + 1))
                    for k in range(4 * b, 4 * b + 4):
                        last = act.activation(XTE[:, buf, k, :], bank[b % 2][:, (k % 4) * P:(k % 4 + 1) * P], ACT.Copy,
                                              scale=GT[:, 48 + k:49 + k])
                    last.then_inc(xte_kept, 1)

            with act.Fori(0, n_rounds) as r:
                keep_tokens(0, r * (4 * PAIRS + 4))
                with act.Fori(0, PAIRS // 2) as i:
                    for p in range(2):
                        for e in range(2):
                            act.wait_ge(w_used, r * ROUND_UNITS + i * (2 * PAIR_UNITS) + (UG + PAIR_UNITS * p + 2 * e + 2))
                            act.activation(SIL[:, e, :, :], bank[2 + e][:, 0:2 * CAP].rearrange("p (f s) -> p f s", f=2),
                                           ACT.Silu).then_inc(silu_ready, 1)
                        keep_tokens(1 - p, r * (4 * PAIRS + 4) + i * 8 + 4 * (p + 1))
                        act.wait_ge(selt_mm, r * PAIRS + i * 2 + (p + 1))
                        act.activation(SELT, bank[3][:, 256:512], ACT.Copy).then_inc(selt_kept, 1)
                        for n in (0, 2):
                            act.wait_ge(y_mm, r * (3 * PAIRS) + i * 6 + (3 * p + n + 1))
                            act.activation(YS[:, n * CH:(n + 1) * CH], bank[4 + n][:, :], ACT.Copy).then_inc(y_act, 1)

            root_mean_square(moe_done, 1, rms_ready)
            keep_norm(4)
            keep_turned(PINT, 0, 256)
            for n in range(4):
                act.wait_ge(w_used, n_rounds * ROUND_UNITS + (UG + 2 * n + 2))
                if n >= 2:
                    act.wait_ge(out_ready, n - 1)
                for t in range(T2):
                    act.activation(XSf[:, (2 * (n % 2) + t) * CH:(2 * (n % 2) + t + 1) * CH],
                                   bank[2 * ((QCH + n) % 2) + t][:, :], ACT.Sigmoid).then_inc(set_free, 1)

        @block.vector
        def _(dve):
            TT, TS, STT = dve.tensor_tensor, dve.tensor_scalar, dve.scalar_tensor_tensor

            def scale_norm(j):
                dve.wait_ge(rms_ready, j + 1)
                dve.reciprocal(rstd, rms)
                dve.drain()
                for t in range(T2):
                    TS(XS[:, t, :], H[:, t, :], rstd[:, t:t + 1], None, ALU.mult).then_inc(xs_ready, 1)
                for k in range(1, KC, 2):
                    dve.wait_ge(x_turned, KC * j + k + 1)
                    TS(XT[:, :, k * P:(k + 1) * P], bank[4 + k % 4][:, 0:256].rearrange("p (t s) -> p t s", t=2),
                       GT[:, 16 * j + k:16 * j + k + 1], None, ALU.mult).then_inc(xt_dve, 1)

            def rope(at, heads):
                x = P1[:, :, at:at + heads * HD].rearrange("p t (h d) -> p t h d", d=HD)
                x1, x2 = x[:, :, :, 0:64], x[:, :, :, 64:128]
                n = 2 * heads * 64
                a, b = (XSf[:, j * 1024:j * 1024 + n].rearrange("p (t h d) -> p t h d", t=2, d=64) for j in range(2))
                c, s = (v.unsqueeze(2).to_broadcast([P, 2, heads, 64]) for v in (cos, sin))
                TT(a, x1, s, ALU.mult)
                TT(b, x2, s, ALU.mult)
                dve.drain()
                TT(x1, x1, c, ALU.mult)
                TT(x2, x2, c, ALU.mult)
                dve.drain()
                TT(x1, x1, b, ALU.subtract)
                return TT(x2, x2, a, ALU.add)

            def prepare(n):
                _, _, _, _, sm, _ = att(n)
                h0, t, nk = group(n)
                dve.wait_ge(scored, n + 1)
                mask = const("wmask" if n < 4 else "cmask")[:, 256 - nk:256]
                for b in range(2):
                    o = sm[:, 2 * b:2 * b + 2, 0:nk]
                    s = bank[4 + b][:, :].rearrange("p (h k) -> p h k", h=2)[:, :, 0:nk]
                    if n < 4:
                        STT(o, s, HD ** -0.5, mask.unsqueeze(1).to_broadcast([P, 2, nk]), ALU.mult, ALU.add)
                    else:
                        for hh in range(2):
                            h = h0 + 2 * b + hh
                            STT(o[:, hh, :], s[:, hh, :], CUM[:, t, h:h + 1], mask, ALU.add, ALU.add)
                dve.drain()
                dve.tensor_reduce(mx, sm[:, :, 0:nk], AX, ALU.max)
                dve.drain()
                if n < 4:
                    TT(mx, mx, sinks[:, h0:h0 + 4], ALU.max)
                    dve.drain()
                    TT(es, sinks[:, h0:h0 + 4], mx, ALU.subtract)
                TS(nmx, mx, -1.0, None, ALU.mult).then_inc(scores_ready, 1)
                dve.wait_ge(exp_ready, 5 * (n + 1))
                if n < 4:
                    TT(rden, rs, es, ALU.add)
                    dve.drain()
                    dve.reciprocal(rden, rden)
                else:
                    dve.reciprocal(rden, rs)
                dve.drain()
                TT(sm[:, :, 0:nk], sm[:, :, 0:nk], rden.unsqueeze(2).to_broadcast([P, 4, nk]), ALU.mult).then_inc(probs_ready, 1)

            dve.sem_inc(set_free, CREDITS)
            dve.wait_ge(c_loaded, 16)
            dve.wait_ge(g_loaded, 10 * 16)
            dve.wait_ge(gt_turned, 1)
            dve.tensor_copy(GT[:, 0:80], bank[4][:, 0:80]).then_inc(gt_ready, 1)
            dve.tensor_copy(GT[:, 80:144], bank[5][:, 0:64]).then_inc(gt_ready, 1)
            dve.wait_ge(gt_ready, 2)
            scale_norm(0)
            dve.wait_ge(rows_loaded, 7 * 16)
            for u in range(UB + 28):
                for step in AFTER1.get(u, ()):
                    if step[0] == "rope":
                        which = step[1]
                        at, heads, chunks = ((QA, 8, 2), (KA, 2, 3), (QR, 8, 5), (KR, 8, 7))[which]
                        dve.wait_ge(set_free, CREDITS + 2 * chunks)
                        last = rope(at, heads)
                        if which >= 2:
                            dve.drain()
                            dec = const("qdecay" if which == 2 else "kdecay")
                        if which == 2:
                            x = P1[:, :, QR:QR + 1024].rearrange("p t (h d) -> p t h d", d=HD)
                            last = TT(x, x, dec.unsqueeze(1).unsqueeze(3).to_broadcast([P, 2, 8, HD]), ALU.mult)
                        if which == 3:
                            x = P1[:, 0, KR:KR + 1024].rearrange("p (h d) -> p h d", d=HD)
                            last = TT(KDEC, x, dec.unsqueeze(2).to_broadcast([P, 8, HD]), ALU.mult)
                        last.then_inc(roped, 1)
                        dve.wait_ge(roped, which + 1)
                    elif step[0] == "S":
                        prepare(step[1])
                    elif step[0] == "R":
                        i = step[1]
                        if i < HEADS:
                            dve.wait_ge(ret_inner, i + 1)
                            dec = const("decay")[:, i * P:(i + 1) * P]
                            TT(IN[:, i % 2, :, :], bank[4][:, 0:256].rearrange("p (t c) -> p t c", t=2),
                               dec.unsqueeze(1).to_broadcast([P, 2, P]), ALU.mult).then_inc(inner_ready, 1)
                        if i:
                            dve.wait_ge(ret_out, i)
                            for t in range(T2):
                                last = dve.bn_stats(STATS[:, 2 * (i - 1) + t, :], bank[6 + (i - 1) % 2][:, t * 256:(t + 1) * 256])
                            last.then_inc(ret_stats, 1)
                    elif step[0] == "rnorm":
                        dve.drain()
                        for g in range(16):
                            last = dve.bn_aggr(MV[:, g, :], STATS[:, g, :])
                        last.then_inc(var_ready, 1)
                        dve.wait_ge(ret_rms, 1)
                        dve.reciprocal(ORSTD, ORMS)
                        dve.wait_ge(ret_kept, HEADS)
                        dve.drain()
                        for g in range(16):
                            o = P1[:, g % 2, VR + 256 * (g // 2):VR + 256 * (g // 2 + 1)]
                            TS(o, o, MV[:, g, 0:1], ORSTD[:, g:g + 1], ALU.subtract, ALU.mult)
                        dve.drain()
                        dve.wait_ge(set_free, CREDITS + 2 * QCB)
                        TT(P1[:, :, GR:GR + D], P1[:, :, VR:VR + D], P1[:, :, GR:GR + D], ALU.mult).then_inc(ret_ready, 1)
                    elif step[0] == "merge":
                        n = step[1]
                        dve.wait_ge(w_used, u + 1)
                        dve.wait_ge(set_free, CREDITS + 2 * (QCB + 2 * n + 2))
                        if n == 0:
                            dve.wait_ge(ret_ready, 1)
                        for t in range(T2):
                            TT(XSf[:, t * CH:(t + 1) * CH], XSf[:, t * CH:(t + 1) * CH], bank[4 + t][:, :], ALU.mult)
                            TT(XSf[:, (2 + t) * CH:(3 + t) * CH], XSf[:, (2 + t) * CH:(3 + t) * CH], bank[6 + t][:, :], ALU.mult)
                        dve.drain()
                        m = P1[:, :, VR + n * CH:VR + (n + 1) * CH]
                        TT(m, XSf[:, 0:1024].rearrange("p (t n) -> p t n", t=2),
                           XSf[:, 1024:2048].rearrange("p (t n) -> p t n", t=2), ALU.add).then_inc(merged, 1)

            def add_square(u0, q0):
                with dve.Fori(0, 2) as i:
                    for c in range(2):
                        dve.wait_ge(w_used, i * 4 + (u0 + 2 * c + 2))
                        for t in range(T2):
                            h = H[:, t, ds(i * (2 * CH) + c * CH, CH)]
                            TT(h, bank[2 * ((q0 + c) % 2) + t][:, :], h, ALU.add).then_inc(set_free, 1)

            add_square(UC, QCC)

            scale_norm(1)
            dve.wait_ge(grow_loaded, 16)
            for t in range(T2):
                TT(HN[:, t, :], XS[:, t, :], GROW, ALU.mult).then_inc(hn_ready, 1)
            def best_keys(t, h0):
                blocks = [(h, q) for h in range(h0, h0 + 4) for q in range(2)]
                dve.wait_ge(s_kept, 4 * t + (h0 + 4) // 2)
                for half in range(2):
                    lo = 8 * half
                    for h, q in blocks:
                        dve.max(TV[:, t, h, q, lo:lo + 8], S[:, t, 2 * h + q, :])
                    dve.drain()
                    for h, q in blocks:
                        dve.max_index(TIU[:, t, h, q, lo:lo + 8], TV[:, t, h, q, lo:lo + 8], S[:, t, 2 * h + q, :])
                    if half == 0:
                        dve.drain()
                        for h, q in blocks:
                            dve.match_replace(S[:, t, 2 * h + q, :], TV[:, t, h, q, 0:8], S[:, t, 2 * h + q, :], LOWEST)
                    dve.drain()
                dve.tensor_copy(TIF[:, t, h0:h0 + 4, :, :], TIU[:, t, h0:h0 + 4, :, :])

            def best_pairs(t, h0):
                hs = slice(h0, h0 + 4)
                TT(CAND[:, hs, :].rearrange("p h (i j) -> p h i j", i=16),
                   TV[:, t, hs, 0, :].unsqueeze(3).to_broadcast([P, 4, 16, 16]),
                   TV[:, t, hs, 1, :].unsqueeze(2).to_broadcast([P, 4, 16, 16]), ALU.add)
                dve.drain()
                for half in range(2):
                    lo = 8 * half
                    for h in range(h0, h0 + 4):
                        dve.max(BV[:, t, h, lo:lo + 8], CAND[:, h, :])
                    dve.drain()
                    for h in range(h0, h0 + 4):
                        dve.max_index(PU[:, 0, h, lo:lo + 8], BV[:, t, h, lo:lo + 8], CAND[:, h, :])
                    if half == 0:
                        dve.drain()
                        for h in range(h0, h0 + 4):
                            dve.match_replace(CAND[:, h, :], BV[:, t, h, 0:8], CAND[:, h, :], LOWEST)
                    dve.drain()
                g = gate_all[:, t, :].rearrange("p (h k) -> p h k", h=8)[:, hs, :]
                TT(g, BV[:, t, hs, :], BV[:, t, hs, 0:1].to_broadcast([P, 4, 16]), ALU.subtract).then_inc(best_ready, 1)
                TS(PU[:, 1, hs, :], PU[:, 0, hs, :], 4, None, ALU.logical_shift_right)
                TS(PU[:, 2, hs, :], PU[:, 0, hs, :], 15, None, ALU.bitwise_and)
                dve.drain()
                dve.tensor_copy(PF[:, 0:2, hs, :], PU[:, 1:3, hs, :])
                dve.drain()
                places = iota[:, 0:16].unsqueeze(1).unsqueeze(1).to_broadcast([P, 4, 16, 16])
                hot = HOT[:, hs, :, :]
                for q in range(2):
                    TT(hot, PF[:, q, hs, :].unsqueeze(3).to_broadcast([P, 4, 16, 16]), places, ALU.is_equal)
                    dve.drain()
                    TT(hot, hot, TIF[:, t, hs, q, :].unsqueeze(2).to_broadcast([P, 4, 16, 16]), ALU.mult)
                    dve.drain()
                    dve.tensor_reduce(PF[:, 2 + q, hs, :], hot, AX, ALU.add)
                    dve.drain()
                STT(idx_all[:, t, :].rearrange("p (h k) -> p h k", h=8)[:, hs, :], PF[:, 2, hs, :], 128.0, PF[:, 3, hs, :],
                    ALU.mult, ALU.add)
                total = gate_sum[:, t, hs]
                dve.wait_ge(gate_exp, 2 * t + h0 // 4 + 1)
                dve.tensor_reduce(total, g, AX, ALU.add)
                dve.drain()
                dve.reciprocal(total, total)
                dve.drain()
                TT(g, g, total.unsqueeze(2).to_broadcast([P, 4, 16]), ALU.mult).then_inc(idx_ready, 1)

            def add_up(t, h, j):
                dve.wait_ge(weight_ready, h * TOPK + (P * t + j + 1))
                dve.wait_ge(up_in[j % 4], h * 64 + 16 * ((P * t + j) // 4 + 1))
                dve.wait_ge(added, h * TOPK + (P * t + j + 4))
                STT(H[:, t, :], W[:, 2 + j % 4 // 2, (j % 2) * D:(j % 2 + 1) * D], wts[:, j:j + 1],
                    H[:, t, :], ALU.mult, ALU.add).then_inc(added, 1)

            def head(t, h):
                for j in range(TOPK):
                    dve.wait_ge(down_in[j % 4], h * 64 + 16 * ((P * t + j) // 4 + 1))
                    dve.wait_ge(dotted, h * TOPK + (P * t + j + 3))
                    dve.tensor_tensor_reduce(out=XT[:, j % 2, :], in0=W[:, j % 4 // 2, (j % 2) * D:(j % 2 + 1) * D],
                                             in1=HN[:, t, :], scale=1.0, scalar=0.0, op0=ALU.mult, op1=ALU.add,
                                             accum_out=dots[:, j:j + 1]).then_inc(dotted, 1)
                    if j >= 2:
                        add_up(t, h, j - 2)
                add_up(t, h, TOPK - 2)
                add_up(t, h, TOPK - 1)

            best_keys(0, 0)
            dve.wait_ge(s_kept, 8)
            best_pairs(0, 0)
            dve.sem_inc(dotted, 4)
            dve.sem_inc(added, 4)
            dve.wait_ge(xt_act, 16)
            for h, (step, t, h0) in enumerate(((best_keys, 0, 4), (best_pairs, 0, 4), (best_keys, 1, 0),
                                               (best_pairs, 1, 0), (best_keys, 1, 4), (best_pairs, 1, 4))):
                head(0, h)
                step(t, h0)
            with dve.Fori(6, HEADS) as h:
                head(0, h)
            with dve.Fori(0, HEADS) as h:
                head(1, h)
            dve.wait_ge(added, 4 + T2 * P)
            dve.sem_inc(peer_done, 1)

            dve.wait_ge(fin_rms, 1)
            dve.reciprocal(rstd, rms)
            dve.wait_ge(grow_loaded, 32)
            dve.drain()
            for t in range(T2):
                STT(H[:, t, :], H[:, t, :], rstd[:, t:t + 1], GROW, ALU.mult, ALU.mult).then_inc(x2_ready, 1)
            dve.wait_ge(x2_ready, 2)
            scale_norm(2)
            dve.memset(RX[:, :, 0:4], 0.0)
            dve.memset(CT, 0.0)
            dve.drain()
            for u in range(20):
                for step in AFTER2.get(u, ()):
                    if step[0] == "FL":
                        dve.wait_ge(fl_done, 1)
                        TT(SPV[:, 0:16].rearrange("p (t h) -> p t h", t=2), bank[4][:, 0:16].rearrange("p (t h) -> p t h", t=2),
                           b_forget.unsqueeze(1).to_broadcast([P, 2, 8]), ALU.add)
                        dve.tensor_copy(SPV[:, 16:24], lam)
                        dve.drain()
                        STT(SPA, SPV, -1.0, SPV, ALU.mult, ALU.max).then_inc(sp_in, 1)
                        dve.wait_ge(sp_exp, 1)
                        TS(SPS, SPZ, 2.0, None, ALU.add)
                        dve.drain()
                        dve.reciprocal(SPS, SPS)
                        dve.drain()
                        TT(SPS, SPS, SPZ, ALU.mult)
                        dve.drain()
                        TT(SPQ, SPS, SPS, ALU.mult)
                        dve.drain()
                        TS(SPA, SPQ, 1.0 / 17.0, None, ALU.mult)
                        for m in (15, 13, 11, 9, 7, 5, 3):
                            dve.drain()
                            STT(SPA, SPA, 1.0 / m, SPQ, ALU.add, ALU.mult)
                        dve.drain()
                        STT(SPA, SPA, 1.0, SPS, ALU.add, ALU.mult)
                        TS(SPV, SPV, -1.0, 0.0, ALU.mult, ALU.max)
                        dve.drain()
                        STT(SPA, SPA, 2.0, SPV, ALU.mult, ALU.add)
                        dve.drain()
                        TS(LF, SPA[:, 0:16].rearrange("p (t h) -> p t h", t=2), -1.0, None, ALU.mult)
                        TS(lru_neg, SPA[:, 16:24], -8.0, None, ALU.mult)
                        TS(lru_pos, SPA[:, 16:24], 8.0, None, ALU.mult)
                        dve.drain()
                        dve.sem_inc(sp_done, 1)
                    elif step[0] == "conv":
                        dve.wait_ge(set_free, CREDITS + 2 * (QCE + 2))
                        for k in (3, 2, 1, 0):
                            for b in range(8):
                                x = RX[:, b, 1 + k:257 + k]
                                if k == 3:
                                    TS(XC[:, b, :], x, conv_w[:, k, b:b + 1], conv_b[:, b:b + 1], ALU.mult, ALU.add)
                                else:
                                    STT(XC[:, b, :], x, conv_w[:, k, b:b + 1], XC[:, b, :], ALU.mult, ALU.add)
                            dve.drain()
                        dve.sem_inc(conv_ready, 1)
                    elif step[0] == "lru":
                        dve.wait_ge(decay_ready, 8)
                        TT(TMP, DECAY_A, DECAY_A, ALU.mult)
                        dve.wait_ge(gates_ready, 16)
                        TT(IGATE, IGATE, XC, ALU.mult)
                        dve.drain()
                        STT(TMP, TMP, 1.0, RGATE, ALU.add, ALU.mult).then_inc(gap_ready, 1)
                        dve.wait_ge(gap_root, 1)
                        TT(IGATE, IGATE, TMP, ALU.mult)
                        dve.drain()
                        for b in range(8):
                            dve.tensor_tensor_scan(TMP[:, b, :], DECAY_A[:, b, :], IGATE[:, b, :], 0.0, ALU.mult, ALU.add)
                        dve.drain()
                    elif step[0] == "gelu":
                        dve.wait_ge(set_free, CREDITS + 2 * QCF)
                        TT(PX.rearrange("p t (b s) -> p b t s", s=P), TMP.rearrange("p b (t s) -> p b t s", t=2),
                           GELU.rearrange("p b (t s) -> p b t s", t=2), ALU.mult).then_inc(rnn_ready, 1)
                    elif step[0] == "FC":
                        dve.wait_ge(cum_done, 1)
                        dve.tensor_copy(CUM, bank[4][:, 0:16].rearrange("p (t h) -> p t h", t=2)).then_inc(cum_kept, 1)
                    elif step[0] == "qknorm":
                        which = step[1]
                        dve.wait_ge(set_free, CREDITS + 2 * (QCE + 4 + 2 * which))
                        x = P2[:, :, which * 1024:(which + 1) * 1024]
                        sq = XSf[:, 0:2048].rearrange("p (t n) -> p t n", t=2)
                        TT(sq, x, x, ALU.mult)
                        dve.drain()
                        dve.tensor_reduce(hrms, sq.rearrange("p t (h d) -> p t h d", d=HD), AX, ALU.add).then_inc(hsq_ready, 1)
                        dve.wait_ge(hrms_ready, which + 1)
                        dve.reciprocal(hrstd, hrms)
                        dve.drain()
                        if which == 0:
                            TS(hrstd, hrstd, HD ** -0.5, None, ALU.mult)
                            dve.drain()
                        xh = x.rearrange("p t (h d) -> p t h d", d=HD)
                        TT(xh, xh, hrstd.unsqueeze(3).to_broadcast([P, 2, 8, HD]), ALU.mult)
                        dve.drain()
                        xg = x.rearrange("p t (h d) -> p (t) h d", d=HD)
                        TT(xg, xg, qk_gain[which].unsqueeze(1).unsqueeze(1).to_broadcast([P, 2, 8, HD]), ALU.mult).then_inc(qk_ready, 1)
                    elif step[0] == "S":
                        prepare(step[1])
            add_square(UF, QCF)

            dve.sem_inc(hid_ready, 2)
            dve.sem_inc(selt_kept, 1)
            dve.sem_inc(scat_added, 8)
            dve.sem_inc(y_act, 2)
            dve.sem_inc(y_dve, 2)
            dve.memset(RL[:, :, 4:8], LOWEST)
            scale_norm(3)
            dve.wait_ge(routed, 1)
            logits = bank[4][:, 0:128].rearrange("p (t e) -> p t e", t=2)
            dve.tensor_copy(RL[:, :, 0:4], logits[:, :, 0:4])
            dve.tensor_copy(RL[:, :, 8:40], logits[:, :, 4:36])
            dve.drain()
            for g in range(2):
                seen = RL[:, :, 0:8] if g == 0 else ML
                for t in range(T2):
                    dve.max(TOPV[:, t, g, :], seen[:, t, :])
                dve.drain()
                for t in range(T2):
                    dve.max_index(TOPU[:, t, g, :], TOPV[:, t, g, :], seen[:, t, :])
                dve.drain()
                dve.tensor_copy(TOPF[:, :, g, :], TOPU[:, :, g, :])
                dve.drain()
                if g == 0:
                    pick, drop = RSC[:, :, 4:8], HOT32[:, :, 0:4]
                    for t in range(T2):
                        TS(pick[:, t, :], iota[:, 0:4], TOPF[:, t, 0, 0:1], None, ALU.is_equal)
                    dve.drain()
                    TS(drop, pick, -1.0, -LOWEST, ALU.add, ALU.mult)
                    m = ML.rearrange("p t (g e) -> p t g e", g=4)
                    TT(m, RL[:, :, 8:40].rearrange("p t (g e) -> p t g e", g=4), pick.unsqueeze(3).to_broadcast([P, 2, 4, 8]), ALU.mult)
                    dve.drain()
                    TT(m, m, drop.unsqueeze(3).to_broadcast([P, 2, 4, 8]), ALU.add)
                    dve.drain()
            for t in range(T2):
                TS(GEXP[:, t, :], RL[:, t, 0:4], TOPV[:, t, 0, 0:1], None, ALU.subtract)
            TT(RSC[:, :, 0:1], TOPV[:, :, 1, 1:2], TOPV[:, :, 1, 0:1], ALU.subtract)
            dve.drain()
            dve.sem_inc(route_in, 1)
            dve.wait_ge(route_exp, 1)
            dve.tensor_reduce(RSC[:, :, 1], GEXP, AX, ALU.add)
            TS(RSC[:, :, 2:3], RSC[:, :, 0:1], 1.0, None, ALU.add)
            dve.drain()
            dve.reciprocal(RSC[:, :, 1:3], RSC[:, :, 1:3])
            dve.drain()
            TT(RSC[:, :, 2:3], RSC[:, :, 2:3], RSC[:, :, 1:2], ALU.mult)
            dve.drain()
            TT(RSC[:, :, 3:4], RSC[:, :, 2:3], RSC[:, :, 0:1], ALU.mult)
            dve.drain()
            for t in range(T2):
                TS(COMB[:, t, :], iota[:, 0:EXPERTS], TOPF[:, t, 1, 0:1], RSC[:, t, 2:3], ALU.is_equal, ALU.mult)
                TS(HOT32[:, t, :], iota[:, 0:EXPERTS], TOPF[:, t, 1, 1:2], RSC[:, t, 3:4], ALU.is_equal, ALU.mult)
            dve.drain()
            TT(COMB, COMB, HOT32, ALU.add)
            for t in range(T2):
                TS(PICK[:, t, 0:EXPERTS], iota[:, 0:EXPERTS], TOPF[:, t, 1, 0:1], None, ALU.is_equal)
            dve.drain()
            for t in range(T2):
                STT(PICK[:, t, 0:EXPERTS], iota[:, 0:EXPERTS], TOPF[:, t, 1, 1:2], PICK[:, t, 0:EXPERTS],
                    ALU.is_equal, ALU.add)
            dve.memset(RANK[:, :, EXPERTS:EXPERTS + 2], -1.0)
            dve.memset(CW[:, :, EXPERTS:EXPERTS + 2], 0.0)
            dve.memset(HID, 0.0)
            dve.drain()
            dve.sem_inc(comb_ready, 1)
            dve.wait_ge(ranked, 1)
            TT(RANK[:, :, 0:EXPERTS], bank[5][:, 0:2 * EXPERTS].rearrange("p (t e) -> p t e", t=2),
               PICK[:, :, 0:EXPERTS], ALU.mult)
            dve.tensor_reduce(most, bank[5][:, 2 * EXPERTS:3 * EXPERTS], AX, ALU.max)
            dve.drain()
            TS(RANK[:, :, 0:EXPERTS], RANK[:, :, 0:EXPERTS], -1.0, None, ALU.add)
            for m in range(1, MAX_ROUNDS):
                TS(over[:, m - 1:m], most, float(m * CAP), None, ALU.is_gt)
            dve.drain()
            dve.tensor_reduce(most, over, AX, ALU.add)
            dve.drain()
            TS(rounds, most, 1.0, None, ALU.add)
            dve.drain()
            dve.sem_inc(rounds_ready, 1)
            n_rounds = dve.value_load(rounds[0:1, 0:1], min_val=1, max_val=MAX_ROUNDS)

            def select(buf, rank, weight, e0):
                for e in range(2):
                    for t in range(T2):
                        TS(SEL[:, buf, t, e * CAP:(e + 1) * CAP], iota, rank[:, t, e0 + e:e0 + e + 1],
                           None, ALU.is_equal)
                        TS(SELW[:, buf, t, e * CAP:(e + 1) * CAP], iota, rank[:, t, e0 + e:e0 + e + 1],
                           weight[:, t, e0 + e:e0 + e + 1], ALU.is_equal, ALU.mult)
                dve.drain()
                dve.sem_inc(sel_ready, 1)

            with dve.Fori(0, n_rounds) as r:
                select(0, RANK, CW, 0)
                with dve.Fori(0, PAIRS // 2) as i:
                    dve.tensor_copy(now_rank, RANK[:, :, ds(i * 4 + 2, 4)])
                    dve.tensor_copy(now_cw, CW[:, :, ds(i * 4 + 2, 4)])
                    dve.drain()
                    for p in range(2):
                        select(1 - p, now_rank, now_cw, 2 * p)
                        for e in range(2):
                            dve.wait_ge(silu_ready, r * EXPERTS + i * 4 + (2 * p + e + 1))
                            TT(HID[:, p, e, :, e * CAP:(e + 1) * CAP], SIL[:, e, :, :],
                               bank[2 + e][:, 2 * CAP:4 * CAP].rearrange("p (f s) -> p f s", f=2), ALU.mult).then_inc(hid_ready, 1)
                        for n in (1, 3):
                            if n == 1:
                                dve.wait_ge(y_mm, r * (3 * PAIRS) + i * 6 + (3 * p + 2))
                            else:
                                dve.wait_ge(w_used, r * ROUND_UNITS + i * (2 * PAIR_UNITS) + (UG + PAIR_UNITS * (p + 1)))
                            dve.tensor_copy(YS[:, n * CH:(n + 1) * CH], bank[4 + n][:, :]).then_inc(y_dve, 1)
                        for n in range(4):
                            for t in range(T2):
                                dve.wait_ge(scat_mm, r * (8 * PAIRS) + i * 16 + (8 * p + 2 * n + t + 1))
                                h = H[:, t, n * CH:(n + 1) * CH]
                                TT(h, bank[t][:, :], h, ALU.add).then_inc(scat_added, 1)
                dve.drain()
                TS(RANK[:, :, :], RANK[:, :, :], -float(CAP), None, ALU.add)
                dve.drain()
            dve.sem_inc(moe_done, 1)

            scale_norm(4)
            for n in range(4):
                dve.wait_ge(set_free, CREDITS + 2 * (QCH + n + 1))
                dve.wait_ge(up_done, n + 1)
                x = XSf[:, 2 * (n % 2) * CH:2 * (n % 2 + 1) * CH].rearrange("p (t n) -> p t n", t=2)
                for t in range(T2):
                    TT(x[:, t, :], x[:, t, :], bank[4 + 2 * (n % 2) + t][:, :], ALU.mult)
                dve.drain()
                h = H[:, :, n * CH:(n + 1) * CH]
                TT(h, h, x, ALU.add).then_inc(out_ready, 1)


def constants():
    import numpy as np

    c = np.zeros((P, CONST_W), np.float32)

    def put(name, value):
        a, b = CONST_AT[name]
        c[:, a:b] = value

    row = np.arange(P)
    put("ident", np.eye(P))
    freq = (1.0 / (np.float32(10000.0) ** (np.arange(0, HD, 2, dtype=np.float32) / np.float32(HD)))).astype(np.float32)
    angle = (np.arange(2 * P, dtype=np.float32)[:, None] * freq[None, :]).astype(np.float32)
    for name, f in (("cos", np.cos), ("sin", np.sin)):
        put(name, f(angle).reshape(2, P, 64).transpose(1, 0, 2).reshape(P, 128))
    causal = np.where(row[None, :] <= row[:, None], 0.0, NEG)
    put("wmask", np.concatenate([np.where(row[None, :] > row[:, None], 0.0, NEG), causal], 1))
    put("cmask", np.concatenate([np.zeros((P, P)), causal], 1))
    gamma = 1.0 - 2.0 ** (-5.0 - np.arange(HEADS))
    lower = row[None, :] >= row[:, None]
    put("decay", np.concatenate([np.where(lower, g ** -(row[:, None] + 1.0) * HD ** -0.5, 0.0) for g in gamma], 1))
    put("qdecay", gamma[None, :] ** (row[:, None] + 1.0))
    put("kdecay", gamma[None, :] ** (P - 1.0 - row[:, None]) * HD ** -0.5)
    put("tri", np.concatenate([row[:, None] <= row[None, :], np.ones((P, P))], 1))
    sel = np.zeros((P, HEADS, P))
    for h in range(HEADS):
        sel[h, h, :] = -1.0
    put("sel", sel.reshape(P, -1))
    put("iota64", np.arange(CAP)[None, :])
    put("eps", EPS)
    return c


INPUTS = ["x", "attn_norm", "w_in", "attn_sinks", "w_attn_branch", "w_ret_branch", "w_out", "ffn_norm",
          "w_peer_query", "peer_sub_keys", "peer_expert_down", "peer_expert_up", "final_norm", "p_2",
          "mix_norm_2", "w_in_2", "b_forget_2", "q_norm_2", "k_norm_2", "conv_w_2", "conv_b_2",
          "w_rec_gate_2", "b_rec_gate_2", "w_in_gate_2", "b_in_gate_2", "lru_lambda_2", "w_out_2",
          "ffn_norm_2", "w_router_group_2", "w_router_expert_2", "w_expert_gate_2", "w_expert_up_2",
          "w_expert_down_2", "ple_norm_2", "w_ple_gate_2", "w_ple_up_2"]


def kernel(**inputs):
    import numpy as np
    import concourse.bacc as bacc
    from concourse.bass_utils import run_bass_kernel_spmd

    nc = bacc.Bacc("TRN2", target_bir_lowering=False, num_devices=1)
    arrays, aps = {}, {}
    for name in INPUTS:
        a = np.ascontiguousarray(inputs[name])
        arrays["in_" + name] = a
        aps[name] = nc.dram_tensor("in_" + name, a.shape, mybir.dt.from_np(a.dtype), kind="ExternalInput").ap()
    arrays["consts"] = constants()
    consts = nc.dram_tensor("consts", (P, CONST_W), mybir.dt.float32, kind="ExternalInput").ap()
    out = nc.dram_tensor("out", (1, 2 * P, D), mybir.dt.float32, kind="ExternalOutput").ap()
    two_blocks(nc, aps, consts, out)
    r = run_bass_kernel_spmd(nc, [arrays], core_ids=[0])
    return r.results[0]["out"]
```
